# Optimizing a Trainium2 kernel written in Bass

```python
import jax, jax.numpy as jnp
from jax import lax
import numpy as np

D_MODEL = 1024
BATCH = 1
SEQ = 512
DEPTH = 2

HEAD_DIM = 64
DIFF_HEADS = 4
DIFF_QK_W = DIFF_HEADS * 2 * HEAD_DIM
DIFF_V_W = DIFF_HEADS * 2 * HEAD_DIM
DIL_HEADS = 8
DIL_W = DIL_HEADS * HEAD_DIM
DIL_PATTERNS = ((128, 1), (512, 4), (2048, 16))
HGRN_HEADS = 4
HGRN_DK = 128
HGRN_DV = 128
HGRN_K_W = HGRN_HEADS * HGRN_DK
HGRN_V_W = HGRN_HEADS * HGRN_DV
HGRN_CHUNK = 64
N_BRANCH = 3
D_FF = 2816
Q_BLOCK = 128
NORM_EPS = 1e-6
N_ALIBI = DIFF_HEADS + DIL_HEADS
ALIBI_A_IDX = (0, 3, 6, 9)
ALIBI_B_IDX = (1, 2, 4, 5, 7, 8, 10, 11)
IN_SIZES = (DIFF_QK_W, DIFF_QK_W, DIFF_V_W, DIL_W, DIL_W, DIL_W,
            HGRN_K_W, HGRN_K_W, HGRN_K_W, HGRN_V_W, HGRN_V_W, N_BRANCH * D_MODEL)
D_IN = sum(IN_SIZES)

kernel_name = "hybrid_diffattn_dilated_hgrn2_gated_encoder"

def rms_norm(x, g):
    xf = x.astype(jnp.float32)
    y = xf * lax.rsqrt(jnp.mean(xf * xf, axis=-1, keepdims=True) + NORM_EPS)
    return (y * g.astype(jnp.float32)).astype(x.dtype)

def swiglu(x, w_gate, w_up, w_down):
    return (jax.nn.silu(x @ w_gate) * (x @ w_up)) @ w_down

def alibi_slopes():
    h = jnp.arange(1, N_ALIBI + 1, dtype=jnp.float32)
    s = jnp.exp2(-8.0 * h / N_ALIBI)
    return s[jnp.array(ALIBI_A_IDX)], s[jnp.array(ALIBI_B_IDX)]

def split_columns(z):
    parts = []
    start = 0
    for size in IN_SIZES:
        parts.append(z[..., start:start + size])
        start += size
    return parts

def diff_attention(q, k, v, slopes, lam, subln, lam_init):
    B, S, H = q.shape[0], q.shape[1], q.shape[2]
    scale = HEAD_DIM ** -0.5
    qh = jnp.transpose(q, (0, 2, 3, 1, 4))
    kh = jnp.transpose(k, (0, 2, 3, 1, 4))
    vh = jnp.transpose(v, (0, 2, 1, 3))
    nblk = S // Q_BLOCK
    qb = jnp.moveaxis(qh.reshape(B, H, 2, nblk, Q_BLOCK, HEAD_DIM), 3, 0)
    kpos = jnp.arange(S)

    def block(args):
        qblk, bi = args
        qpos = bi * Q_BLOCK + jnp.arange(Q_BLOCK)
        dist = jnp.abs(qpos[:, None] - kpos[None, :]).astype(jnp.float32)
        bias = -slopes[:, None, None] * dist
        s = jnp.einsum('bhmqd,bhmkd->bhmqk', qblk, kh).astype(jnp.float32) * scale
        p = jax.nn.softmax(s + bias[None, :, None], axis=-1)
        pd = p[:, :, 0] - lam * p[:, :, 1]
        return jnp.einsum('bhqk,bhkv->bhqv', pd.astype(vh.dtype), vh)

    o = lax.map(block, (qb, jnp.arange(nblk)))
    o = jnp.moveaxis(o, 0, 2).reshape(B, H, S, 2 * HEAD_DIM)
    o = (rms_norm(o, subln) * (1.0 - lam_init)).astype(q.dtype)
    return jnp.transpose(o, (0, 2, 1, 3)).reshape(B, S, H * 2 * HEAD_DIM)

def dilated_pattern(q, k, v, slopes, window, dilation):
    B, H, S, dh = q.shape
    R = window // (2 * dilation)
    L = S // dilation
    nb = -(-L // R)
    Lp = nb * R
    scale = dh ** -0.5

    def to_sub(t):
        return jnp.swapaxes(t.reshape(B, H, L, dilation, dh), 2, 3)

    qs = jnp.pad(to_sub(q), ((0, 0), (0, 0), (0, 0), (0, Lp - L), (0, 0)))
    qs = qs.reshape(B, H, dilation, nb, R, dh)

    def band(t):
        tp = jnp.pad(to_sub(t), ((0, 0), (0, 0), (0, 0), (R, Lp - L + R), (0, 0)))
        tb = tp.reshape(B, H, dilation, nb + 2, R, dh)
        return jnp.concatenate([tb[:, :, :, :-2], tb[:, :, :, 1:-1], tb[:, :, :, 2:]], axis=4)

    kb, vb = band(k), band(v)
    qi = jnp.arange(nb)[:, None] * R + jnp.arange(R)[None, :]
    ki = jnp.arange(nb)[:, None] * R + jnp.arange(3 * R)[None, :] - R
    rel = jnp.abs(qi[:, :, None] - ki[:, None, :])
    valid = (rel <= R) & (ki[:, None, :] >= 0) & (ki[:, None, :] < L)
    bias = -slopes[:, None, None, None] * (rel * dilation).astype(jnp.float32)
    s = jnp.einsum('bhrnqd,bhrnkd->bhrnqk', qs, kb).astype(jnp.float32) * scale + bias[None, :, None]
    s = jnp.where(valid, s, -jnp.inf)
    lse = jax.nn.logsumexp(s, axis=-1)
    p = jnp.exp(s - lse[..., None])
    o = jnp.einsum('bhrnqk,bhrnkd->bhrnqd', p.astype(v.dtype), vb)
    o = o.reshape(B, H, dilation, Lp, dh)[:, :, :, :L]
    lse = lse.reshape(B, H, dilation, Lp)[:, :, :, :L]
    o = jnp.swapaxes(o, 2, 3).reshape(B, H, S, dh)
    lse = jnp.swapaxes(lse, 2, 3).reshape(B, H, S)
    return o, lse

def dilated_attention(q, k, v, slopes):
    B, S, _ = q.shape
    heads = lambda t: jnp.transpose(t.reshape(B, S, DIL_HEADS, HEAD_DIM), (0, 2, 1, 3))
    qh, kh, vh = heads(q), heads(k), heads(v)
    outs, lses = [], []
    for window, dilation in DIL_PATTERNS:
        o, lse = dilated_pattern(qh, kh, vh, slopes, window, dilation)
        outs.append(o)
        lses.append(lse)
    wts = jax.nn.softmax(jnp.stack(lses, axis=0), axis=0)
    o = jnp.einsum('pbhs,pbhsd->bhsd', wts, jnp.stack(outs, axis=0).astype(jnp.float32))
    return jnp.transpose(o, (0, 2, 1, 3)).reshape(B, S, DIL_W).astype(q.dtype)

def gla_chunk_scan(q, k, v, g):
    B, H, S, dk = q.shape
    dv = v.shape[-1]
    C = HGRN_CHUNK
    n = S // C
    chunks = lambda t: jnp.moveaxis(t.reshape(B, H, n, C, t.shape[-1]), 2, 0)
    causal = jnp.tril(jnp.ones((C, C), dtype=bool))

    def step(state, inp):
        qc, kc, vc, gc = inp
        bc = jnp.cumsum(gc, axis=2)
        o_inter = jnp.einsum('bhck,bhkv->bhcv', qc * jnp.exp(bc), state)
        diff = bc[:, :, :, None, :] - bc[:, :, None, :, :]
        decay = jnp.exp(jnp.where(causal[:, :, None], diff, -jnp.inf))
        a = jnp.einsum('bhtk,bhsk,bhtsk->bhts', qc, kc, decay)
        o_intra = jnp.einsum('bhts,bhsv->bhtv', a, vc)
        btot = bc[:, :, -1]
        state = jnp.exp(btot)[..., None] * state + jnp.einsum(
            'bhck,bhcv->bhkv', kc * jnp.exp(btot[:, :, None] - bc), vc)
        return state, o_inter + o_intra

    s0 = jnp.zeros((B, H, dk, dv), jnp.float32)
    _, o = lax.scan(step, s0, (chunks(q), chunks(k), chunks(v), chunks(g)))
    return jnp.moveaxis(o, 0, 2).reshape(B, H, S, dv)

def hgrn_direction(q, f_logit, i, lb):
    g = jnp.log(lb + (1.0 - lb) * jax.nn.sigmoid(f_logit))
    k = (1.0 - lb) * jax.nn.sigmoid(-f_logit)
    return gla_chunk_scan(q, k, i, g)

def hgrn2_mixer(q, f_fw, f_bw, i, og, lb, norm_g):
    B, S, _ = q.shape
    heads = lambda t, d: jnp.transpose(t.reshape(B, S, HGRN_HEADS, d), (0, 2, 1, 3)).astype(jnp.float32)
    qh, ih = heads(q, HGRN_DK), heads(i, HGRN_DV)
    ffh, fbh = heads(f_fw, HGRN_DK), heads(f_bw, HGRN_DK)
    lbh = lb.astype(jnp.float32).reshape(HGRN_HEADS, 1, HGRN_DK)
    o_fw = hgrn_direction(qh, ffh, ih, lbh)
    rev = lambda t: jnp.flip(t, axis=2)
    o_bw = rev(hgrn_direction(rev(qh), rev(fbh), rev(ih), lbh))
    o = rms_norm(o_fw + o_bw, norm_g) * jax.nn.silu(heads(og, HGRN_DV))
    return jnp.transpose(o, (0, 2, 1, 3)).reshape(B, S, HGRN_V_W).astype(q.dtype)

def setup_inputs(seed: int = 0) -> dict:
    key = jax.random.key(seed)
    ks = jax.random.split(key, 24)
    f32 = jnp.float32
    dense = lambda k, shape, fan_in: jax.random.normal(k, shape, f32) * fan_in ** -0.5
    gain = lambda k, shape: 1.0 + 0.02 * jax.random.normal(k, shape, f32)
    return {
        "x": jax.random.normal(ks[0], (BATCH, SEQ, D_MODEL), f32),
        "ffn1_norm": gain(ks[1], (DEPTH, D_MODEL)),
        "ffn1_w_gate": dense(ks[2], (DEPTH, D_MODEL, D_FF), D_MODEL),
        "ffn1_w_up": dense(ks[3], (DEPTH, D_MODEL, D_FF), D_MODEL),
        "ffn1_w_down": dense(ks[4], (DEPTH, D_FF, D_MODEL), D_FF),
        "mix_norm": gain(ks[5], (DEPTH, D_MODEL)),
        "w_in": dense(ks[6], (DEPTH, D_MODEL, D_IN), D_MODEL),
        "diff_lambda_q1": 0.1 * jax.random.normal(ks[7], (DEPTH, HEAD_DIM), f32),
        "diff_lambda_k1": 0.1 * jax.random.normal(ks[8], (DEPTH, HEAD_DIM), f32),
        "diff_lambda_q2": 0.1 * jax.random.normal(ks[9], (DEPTH, HEAD_DIM), f32),
        "diff_lambda_k2": 0.1 * jax.random.normal(ks[10], (DEPTH, HEAD_DIM), f32),
        "diff_subln": gain(ks[11], (DEPTH, 2 * HEAD_DIM)),
        "hgrn_lower_bounds": 0.1 * jax.random.normal(ks[12], (DEPTH, HGRN_K_W), f32),
        "hgrn_norm": gain(ks[13], (DEPTH, HGRN_DV)),
        "w_branch_a": dense(ks[14], (DEPTH, DIFF_V_W, D_MODEL), DIFF_V_W),
        "w_branch_b": dense(ks[15], (DEPTH, DIL_W, D_MODEL), DIL_W),
        "w_branch_c": dense(ks[16], (DEPTH, HGRN_V_W, D_MODEL), HGRN_V_W),
        "w_out": dense(ks[17], (DEPTH, D_MODEL, D_MODEL), D_MODEL),
        "ffn2_norm": gain(ks[18], (DEPTH, D_MODEL)),
        "ffn2_w_gate": dense(ks[19], (DEPTH, D_MODEL, D_FF), D_MODEL),
        "ffn2_w_up": dense(ks[20], (DEPTH, D_MODEL, D_FF), D_MODEL),
        "ffn2_w_down": dense(ks[21], (DEPTH, D_FF, D_MODEL), D_FF),
        "final_norm": gain(ks[22], (D_MODEL,)),
    }

def reference(x, ffn1_norm, ffn1_w_gate, ffn1_w_up, ffn1_w_down, mix_norm, w_in,
              diff_lambda_q1, diff_lambda_k1, diff_lambda_q2, diff_lambda_k2, diff_subln,
              hgrn_lower_bounds, hgrn_norm, w_branch_a, w_branch_b, w_branch_c, w_out,
              ffn2_norm, ffn2_w_gate, ffn2_w_up, ffn2_w_down, final_norm):
    B, S, _ = x.shape
    slopes_a, slopes_b = alibi_slopes()
    lb_p = jax.nn.softmax(hgrn_lower_bounds.astype(jnp.float32), axis=0)
    lb_all = jnp.cumsum(lb_p, axis=0) - lb_p[0]
    h = x
    for l in range(DEPTH):
        h = h + 0.5 * swiglu(rms_norm(h, ffn1_norm[l]), ffn1_w_gate[l], ffn1_w_up[l], ffn1_w_down[l])
        u = rms_norm(h, mix_norm[l])
        z = u @ w_in[l]
        a_q, a_k, a_v, b_q, b_k, b_v, c_q, c_ffw, c_fbw, c_i, c_og, gates = split_columns(z)
        lam_init = 0.8 - 0.6 * float(np.exp(-0.3 * l))
        lam = (jnp.exp(jnp.sum(diff_lambda_q1[l] * diff_lambda_k1[l]).astype(jnp.float32))
               - jnp.exp(jnp.sum(diff_lambda_q2[l] * diff_lambda_k2[l]).astype(jnp.float32)) + lam_init)
        ya = diff_attention(a_q.reshape(B, S, DIFF_HEADS, 2, HEAD_DIM),
                            a_k.reshape(B, S, DIFF_HEADS, 2, HEAD_DIM),
                            a_v.reshape(B, S, DIFF_HEADS, 2 * HEAD_DIM),
                            slopes_a, lam, diff_subln[l], lam_init)
        yb = dilated_attention(b_q, b_k, b_v, slopes_b)
        yc = hgrn2_mixer(c_q, c_ffw, c_fbw, c_i, c_og, lb_all[l], hgrn_norm[l])
        g = jax.nn.sigmoid(gates.astype(jnp.float32)).reshape(B, S, N_BRANCH, D_MODEL).astype(h.dtype)
        merged = (g[:, :, 0] * (ya @ w_branch_a[l]) + g[:, :, 1] * (yb @ w_branch_b[l])
                  + g[:, :, 2] * (yc @ w_branch_c[l]))
        h = h + merged @ w_out[l]
        h = h + 0.5 * swiglu(rms_norm(h, ffn2_norm[l]), ffn2_w_gate[l], ffn2_w_up[l], ffn2_w_down[l])
    return rms_norm(h, final_norm)


_drawn_inputs = setup_inputs


def setup_inputs(seed=0):
    import zlib

    import numpy as np

    out = dict(_drawn_inputs(seed))
    spreads = {}
    factors = {'ffn1_norm': 3.486,
     'diff_lambda_q2': 5.358,
     'diff_subln': 17.19,
     'hgrn_norm': 22.664,
     'ffn2_norm': 5.394,
     'final_norm': 7.98,
     'hgrn_lower_bounds': 3.149}
    for name, (base, spread) in spreads.items():
        noise = np.random.default_rng([zlib.crc32(name.encode()), seed]).standard_normal(out[name].shape)
        drawn = base * np.exp(spread * noise) if base else spread * noise
        out[name] = __import__('jax').numpy.asarray(drawn.astype(out[name].dtype))
    for name, factor in factors.items():
        out[name] = (out[name] * factor).astype(out[name].dtype)
    return out
```

```python
import concourse.bass as bass
from concourse import mybir
import numpy as np

F32 = mybir.dt.float32
F32R = mybir.dt.float32r
U8 = mybir.dt.uint8
BF16 = mybir.dt.bfloat16
ALU = mybir.AluOpType
ACT = mybir.ActivationFunctionType
AX = mybir.AxisListType

DEPTH, D, SEQ, DFF = 2, 1024, 512, 2816
P = 128
KD = D // P
KF = DFF // P
TT_ = SEQ // P
HALF = KF // 2
BRK = 512 // P
MB = KD + BRK
SLOT = MB * P
EPS = 1e-6
CS = 64
NC = SEQ // CS
LEVELS = (32, 16, 8, 4, 2, 1)
F_CAP = 43.6
SCALE = 64 ** -0.5
BASE = 1152
UW = 896

GU = (0, 136)
DN = (44, 180)
C_P1 = 60
C_P2 = 80
C_P3 = 96
C_P4 = 112
C_P5 = 120
C_P6 = 128
CH = 196

G_FFN1, G_MIX, G_FFN2, G_SUB, G_HG, LB, OMLB, NLAM, NPAR = 0, 8, 16, 24, 25, 26, 30, 34, 36


def build(nc, xT, wgu, wdn, wproj, wmerge, wout, gains, final_g, lb_raw, lam_in, ident_c, masks_c,
          bias_c, h_save, out):
    from contextlib import ExitStack
    ctx = ExitStack()
    with ctx:
        def at(name, words, offset, dt=F32):
            return nc.alloc_sbuf_tensor_at(name, [P, words], dt, offset=BASE + offset)

        def tiles(t, n=SEQ):
            return t[:, :].rearrange("p (a n) -> p a n", n=n)

        KB = 1024
        raw = tiles(at("raw", 4 * SLOT, 0), SLOT)
        w_hi = tiles(at("w_hi", 2 * SLOT, 24 * KB, F32R), SLOT)
        w_lo = tiles(at("w_lo", 2 * SLOT, 36 * KB, F32R), SLOT)
        x_hi = tiles(at("x_hi", KD * SEQ, 48 * KB, F32R))
        x_lo = tiles(at("x_lo", KD * SEQ, 64 * KB, F32R))
        HB = 80 * KB
        h = tiles(at("h", KD * SEQ, HB))
        ZB = 96 * KB
        zs = lambda s: ZB + 2 * KB * s
        z = tiles(at("z", 52 * SEQ, ZB))
        CB = zs(52)
        SB = CB + 6 * KB
        mask_f = tiles(at("mask_f", len(LEVELS) * P, zs(40)), P)
        act_hi = tiles(at("act_hi", KF * SEQ, zs(0), F32R))
        act_lo = tiles(at("act_lo", KF * SEQ, zs(22), F32R))
        silu_g = tiles(at("silu_g", 2 * SEQ, zs(44)))
        act_f = tiles(at("act_f", 2 * SEQ, zs(46)))
        x_f = tiles(at("x_f", 2 * SEQ, zs(48)))
        h_sq = tiles(at("h_sq", KD * SEQ, SB))
        ya_hi = tiles(at("ya_hi", 4 * SEQ, zs(0), F32R))
        ya_lo = tiles(at("ya_lo", 4 * SEQ, zs(4), F32R))
        yc_hi = tiles(at("yc_hi", 4 * SEQ, zs(8), F32R))
        yc_lo = tiles(at("yc_lo", 4 * SEQ, zs(12), F32R))
        yb_hi = tiles(at("yb_hi", 4 * SEQ, zs(20), F32R))
        yb_lo = tiles(at("yb_lo", 4 * SEQ, zs(24), F32R))
        merged = tiles(at("merged", KD * SEQ, zs(44)))
        m_hi = tiles(at("m_hi", KD * SEQ, zs(28), F32R))
        m_lo = tiles(at("m_lo", KD * SEQ, zs(36), F32R))
        o_f = at("o_f", SEQ, zs(16))
        o_sq = at("o_sq", SEQ, zs(17))
        gate_t = at("gate_t", SEQ, zs(18))
        gated = at("gated", SEQ, zs(19))
        S = at("S", 8 * SEQ, HB)[:, :].rearrange("p (m t n) -> p m t n", m=2, n=SEQ)
        pT_a = tiles(at("pT_a", 4 * SEQ, HB + 8 * KB))
        pT_b = at("pT_b", 8 * SEQ, zs(8))[:, :].rearrange("p (m t n) -> p m t n", m=2, n=SEQ)
        bias = tiles(at("bias", 2 * UW, SB), UW)
        q_st = at("q_st", SEQ, SB + 7 * KB)
        k_st = at("k_st", SEQ, SB + 9 * KB)
        v_st = at("v_st", SEQ, SB + 11 * KB)
        v_tok = at("v_tok", SEQ, SB + 13 * KB)
        nf = tiles(at("nf", 2 * SEQ, HB))
        kk = tiles(at("kk", 2 * SEQ, HB + 4 * KB))
        ln1 = tiles(at("ln1", 2 * SEQ, HB + 8 * KB))
        gg = tiles(at("gg", 2 * SEQ, HB + 12 * KB))
        xy = [nf, ln1]
        run = tiles(at("run", 2 * SEQ, zs(36)))
        qk64 = tiles(at("qk64", 4 * SEQ, zs(38)))
        k_sum = at("k_sum", SEQ, zs(42))
        og_t = at("og_t", SEQ, zs(43))
        qkl = [tiles(at(f"qkl{b}", 2 * SEQ, zs(44 + 2 * b))) for b in range(2)]
        q_far = tiles(at("q_far", 6 * P, zs(48)), P)
        hq = at("hq", SEQ, zs(50))
        hi_st = at("hi_st", SEQ, zs(51))
        AT_ = at("AT", 5 * SEQ, SB)
        AT = tiles(AT_)
        ATd = tiles(AT_, SEQ + P)[:, :, 0:P]
        i_tok = at("i_tok", SEQ, SB + 10 * KB)
        ho_f = at("ho_f", SEQ, SB + 12 * KB)
        ho_sq = at("ho_sq", SEQ, SB + 14 * KB)
        ident = at("ident", P, CB)
        ones = at("ones", P, CB + 512)
        masks = tiles(at("masks", len(LEVELS) * SEQ, CB + 1 * KB, U8))
        run_mask = at("run_mask", SEQ, CB + 4 * KB, BF16)
        par2 = at("par2", DEPTH * NPAR, CB + 5 * KB)
        small = at("small", 160, CB + 5 * KB + 320)
        par = small[:, 0:36]
        ms, rt, rs = small[:, 36:40], small[:, 40:44], small[:, 44:48]
        neg_max, p_sum, p_rs, p_c2 = small[:, 48:56], small[:, 56:64], small[:, 64:72], small[:, 72:76]
        lb_h = small[:, 76:78]
        tot, ttot = small[:, 80:96], small[:, 96:104]
        fin_g = small[:, 104:112]
        lbr, lbt, lamp = small[:, 112:120], small[:, 120:132], small[:, 132:152]

        bank = [ctx.enter_context(nc.psum_tensor(f"bank{b}", [P, SEQ], F32)) for b in range(8)]

        names = """x_in par_in const_in lo_done chunk_done prod_taken silu_done act_ready h_upd
            sq_ready n_stat n_ms n_rt n_rc n_bc xf_ready xhi_ready xn_ready h_saved h_back out_done
            pre_lam pre_exp par_ready gate_done
            hg_stage hg_it hg_itok hg_nf hg_ln hg_ar hg_kexp hg_rem hg_e hg_ks hg_q64 hg_q128
            hg_og lv_sub lv_exp lv_mul lev_mm lev_taken od_mm od_taken hg_pv hg_sq hg_st hg_ms
            hg_rt hg_rc hg_bc hg_out out_ready gate_ready m_ready""".split()
        sem = {n: ctx.enter_context(nc.semaphore(n)) for n in names}
        raw_in = [ctx.enter_context(nc.semaphore(f"raw_in{s}")) for s in range(4)]
        att = {b: {n: ctx.enter_context(nc.semaphore(f"{n}_{b}")) for n in
                   "tbl stage vt vtok sc ttr exp pd tr pt pv osq st ms rt rc bc out".split()} for b in "ab"}
        X = type("Sems", (), sem)


        def loaded(l, base, i, c):
            return ((l * (CH // 4) + i) + (base // 4 + 1)) * 16

        block = ctx.enter_context(nc.Block())

        @block.sync
        def _(sp):
            sp.dma_start(small[:, 104:112], final_g[:, :]).then_inc(X.par_in, 16)
            sp.dma_start(h[:, :, :], xT.rearrange("(k p) n -> p k n", p=P)).then_inc(X.x_in, 16)

            def chunk(l, base, i, c, src, row, words):
                n = l * CH + (base + c) + i * 4
                sp.wait_ge(X.lo_done, n + 1)
                sp.dma_start(raw[:, c, 0:words], src[bass.ds(row, 1), :, :].rearrange("a p n -> (a p) n"))\
                    .then_inc(raw_in[c], 16)

            def ffn(l, s):
                with sp.Fori(0, KF // 2) as i:
                    for c in range(4):
                        chunk(l, GU[s], i, c, wgu, l * 88 + i * 4 + (44 * s + c), D)
                with sp.Fori(0, KD // 2) as i:
                    for c in range(4):
                        chunk(l, DN[s], i, c, wdn, l * 32 + i * 4 + (16 * s + c), HALF * P)

            with sp.Fori(0, DEPTH) as l:
                ffn(l, 0)
                with sp.Fori(0, 9) as i:
                    for c in range(4):
                        chunk(l, C_P1, i, c, wproj, l * 44 + i * 4 + c, D)
                with sp.Fori(0, 4) as i:
                    chunk(l, C_P3, i, 0, wproj, l * 44 + i * 2 + 36, D)
                    chunk(l, C_P3, i, 1, wmerge, l * 24 + i * 2, SLOT)
                    chunk(l, C_P3, i, 2, wproj, l * 44 + i * 2 + 37, D)
                    chunk(l, C_P3, i, 3, wmerge, l * 24 + i * 2 + 1, SLOT)
                with sp.Fori(0, 4) as i:
                    for c in range(4):
                        chunk(l, C_P4, i, c, wmerge, l * 24 + i * 4 + (8 + c), SLOT)
                with sp.Fori(0, 2) as i:
                    for c in range(4):
                        chunk(l, C_P6, i, c, wout, l * 8 + i * 4 + c, D)
                ffn(l, 1)
            for k in range(KD):
                sp.wait_ge(X.out_ready, k + 1)
                sp.dma_start(out[k * P:(k + 1) * P, :], h_sq[:, k, :]).then_inc(X.out_done, 16)
            sp.wait_ge(X.out_done, 16 * KD)

        @block.gpsimd
        def _(pool):
            pool.sem_inc(X.lo_done, 4)

            def split(l, base, i, c, words):
                n = l * CH + (base + c) + i * 4
                pool.wait_ge(raw_in[c], loaded(l, base, i, c))
                pool.wait_ge(X.chunk_done, n + 1)
                pool.nop(nofuse=True)
                w, hi, lo = raw[:, c, 0:words], w_hi[:, c % 2, 0:words], w_lo[:, c % 2, 0:words]
                nc.gpsimd.tensor_scalar(hi, w, 1.0, 0.0, ALU.mult, ALU.add)
                pool.drain()
                nc.gpsimd.tensor_tensor(lo, w, hi.bitcast(F32), ALU.subtract).then_inc(X.lo_done, 1)

            def ffn(l, s):
                with pool.Fori(0, KF // 2) as i:
                    for c in range(4):
                        split(l, GU[s], i, c, D)
                with pool.Fori(0, KD // 2) as i:
                    for c in range(4):
                        split(l, DN[s], i, c, HALF * P)

            with pool.Fori(0, DEPTH) as l:
                ffn(l, 0)
                with pool.Fori(0, 9) as i:
                    for c in range(4):
                        split(l, C_P1, i, c, D)
                with pool.Fori(0, 4) as i:
                    for c in range(4):
                        split(l, C_P3, i, c, SLOT if c % 2 else D)
                with pool.Fori(0, 4) as i:
                    for c in range(4):
                        split(l, C_P4, i, c, SLOT)
                with pool.Fori(0, 2) as i:
                    for c in range(4):
                        split(l, C_P6, i, c, D)
                ffn(l, 1)

        @block.tensor
        def _(pe):
            pe.sem_inc(X.chunk_done, 2)
            for b in "ab":
                pe.sem_inc(att[b]["sc"], 1)
            mm = nc.tensor.matmul

            def block_products(dst, c, blocks, xh, xl, start, stop):
                for b, k in blocks:
                    w1, w2 = w_hi[:, c % 2, b * P:(b + 1) * P], w_lo[:, c % 2, b * P:(b + 1) * P]
                    first, last = start and b == blocks[0][0], stop and b == blocks[-1][0]
                    mm(dst[:, :], w1, xh(k), start=first, stop=False)
                    mm(dst[:, :], w1, xl(k), start=False, stop=False)
                    m = mm(dst[:, :], w2, xh(k), start=False, stop=last)
                return m

            def weights(l, base, i, c, lag):
                n = l * CH + (base + c) + i * 4
                pe.wait_ge(X.lo_done, n + 5)
                if lag:
                    pe.wait_ge(X.prod_taken, n + 5 - lag)

            def phase_start(l, base):
                pe.wait_ge(X.prod_taken, l * CH + base + 4)
                pe.nop(nofuse=True)

            xh, xl = (lambda k: x_hi[:, k, :]), (lambda k: x_lo[:, k, :])

            def product(l, base, i, c, dst, lag=4):
                weights(l, base, i, c, lag)
                block_products(dst, c, [(k, k) for k in range(KD)], xh, xl, True, True)\
                    .then_inc(X.chunk_done, 1)

            def merge(l, base, i, c, gate_bank, branch_bank, yh, yl):
                weights(l, base, i, c, 2)
                block_products(gate_bank, c, [(k, k) for k in range(KD)], xh, xl, True, True)
                block_products(branch_bank, c, [(KD + k, k) for k in range(BRK)],
                               lambda k: yh[:, k, :], lambda k: yl[:, k, :], True, True)\
                    .then_inc(X.chunk_done, 1)

            def token_sums(sq_tile, n, dst):
                for t in range(TT_):
                    for k in range(n):
                        m = mm(dst[:, t:t + 1], sq_tile(k)[:, t * P:(t + 1) * P], ones[:, 0:1],
                               start=(k == 0), stop=(k == n - 1))
                return m

            def spread(dst):
                for t in range(TT_):
                    m = mm(dst[:, t * P:(t + 1) * P], rs[:, t:t + 1].broadcast_to([P, P]), ident[:, :],
                           start=True, stop=True)
                return m

            def norm(nu):
                pe.wait_ge(X.sq_ready, nu * KD + KD)
                token_sums(lambda k: h_sq[:, k, :], KD, bank[7]).then_inc(X.n_stat, 1)
                pe.wait_ge(X.n_rc, nu + 1)
                spread(bank[6]).then_inc(X.n_bc, 1)

            def ffn(l, s):
                phase_start(l, GU[s])
                with pe.Fori(0, KF // 2) as i:
                    for c in range(4):
                        weights(l, GU[s], i, c, 4)
                        for k in range(KD):
                            if c == 0:
                                pe.wait_ge(X.xn_ready, l * 24 + (16 * s + k + 1))
                            m = block_products(bank[c], c, [(k, k)], xh, xl, k == 0, k == KD - 1)
                        m.then_inc(X.chunk_done, 1)
                with pe.Fori(0, KD // 2) as i:
                    for c in range(4):
                        weights(l, DN[s], i, c, 0 if c % 2 else 4)
                        pe.wait_ge(X.act_ready, l * 44 + (22 * s + (HALF, KF)[c % 2]))
                        block_products(bank[c - c % 2], c, [(k, (c % 2) * HALF + k) for k in range(HALF)],
                                       lambda k: act_hi[:, k, :], lambda k: act_lo[:, k, :],
                                       c % 2 == 0, c % 2 == 1).then_inc(X.chunk_done, 1)

            def transposes(dst, src):
                for b in range(4):
                    m = nc.tensor.transpose(dst[:, b * P:(b + 1) * P], src[:, b * P:(b + 1) * P], ident[:, :])
                return m

            def scores(a, u):
                pe.wait_ge(a["out"], u + 1)
                pe.wait_ge(a["stage"], u + 1)
                transposes(bank[6], v_st).then_inc(a["vt"], 1)
                for g in range(8):
                    m, t = divmod(g, 4)
                    if g >= 2:
                        pe.wait_ge(a["ttr"], u * 8 + (g - 1) + 1)
                    r = slice(64 * m, 64 * m + 64)
                    mm(bank[4 + g % 2][:, :], q_st[r, t * P:(t + 1) * P], k_st[r, :], start=True, stop=True)\
                        .then_inc(a["sc"], 1)

            pe.wait_ge(X.const_in, 32)
            pe.wait_ge(X.pre_lam, 1)
            mm(bank[7][:, 0:4], ones[0:64, :], lamp[0:64, 8:12], start=True, stop=True).then_inc(X.pre_exp, 1)

            with pe.Fori(0, DEPTH) as l:
                norm(l * 3)
                ffn(l, 0)
                norm(l * 3 + 1)
                phase_start(l, C_P1)
                pe.wait_ge(X.xn_ready, l * 24 + 16)
                pe.nop(nofuse=True)
                with pe.Fori(0, 5) as i:
                    for c in range(4):
                        product(l, C_P1, i, c, bank[c])
                phase_start(l, C_P2)
                with pe.Fori(0, 4) as i:
                    u = l * 4 + i
                    product(l, C_P2, i, 0, bank[0])
                    pe.wait_ge(X.hg_stage, u + 1)
                    transposes(bank[6], hi_st).then_inc(X.hg_it, 1)
                    product(l, C_P2, i, 1, bank[1])
                    product(l, C_P2, i, 2, bank[2])
                    pe.wait_ge(X.hg_out, u + 1)

                    def level(n, lhs, rhs):
                        pe.wait_ge(X.lev_taken, u * 8 + (n + 1))
                        b = bank[4 + n % 2]
                        for t in range(TT_):
                            r = slice(t * P, (t + 1) * P)
                            m = mm(b[:, r], lhs[:, r], rhs[:, r], start=True, stop=True)
                        m.then_inc(X.lev_mm, 1)

                    pe.wait_ge(X.hg_ks, u + 1)
                    level(0, k_sum, hq)
                    pe.wait_ge(X.hg_q64, u + 1)
                    pe.wait_ge(X.lev_taken, u * 8 + 2)
                    for t in range(TT_):
                        a, b = slice(t * P, t * P + CS), slice(t * P + CS, (t + 1) * P)
                        mm(bank[5][0:CS, b], qk64[:, 2, a], qk64[:, 0, b], start=True, stop=True)
                        m = mm(bank[5][CS:P, a], qk64[:, 3, b], qk64[:, 1, a], start=True, stop=True)
                    m.then_inc(X.lev_mm, 1)
                    pe.wait_ge(X.hg_q128, u + 1)
                    pe.wait_ge(X.hg_itok, u + 1)
                    sl = lambda t: slice(t * P, (t + 1) * P)
                    far = {(0, 2): 0, (1, 3): 1, (0, 3): 2, (3, 1): 3, (2, 0): 4, (3, 0): 5}
                    for a in range(4):
                        if a >= 2:
                            pe.wait_ge(X.od_taken, u * 4 + (a - 1))
                        for b in range(4):
                            if a != b:
                                rhs = q_far[:, far[a, b], :] if (a, b) in far else qk64[:, int(a > b), sl(b)]
                                m = mm(bank[6 + a % 2][:, sl(b)], qk64[:, 2 + int(a > b), sl(a)], rhs,
                                       start=True, stop=True)
                        m.then_inc(X.od_mm, 1)
                    for j in range(len(LEVELS)):
                        if j == 2:
                            product(l, C_P2, i, 3, bank[3])
                        pe.wait_ge(X.lv_mul, u * 6 + (j + 1) + 1)
                        level(j + 2, qkl[j % 2][:, 1, :], qkl[j % 2][:, 0, :])
                    pe.wait_ge(X.od_taken, u * 4 + 4)
                    pe.wait_ge(X.lev_taken, u * 8 + 10)
                    for a in range(4):
                        m = mm(bank[6][:, :], i_tok[:, sl(a)], AT[:, a, :], start=(a == 0), stop=(a == 3))
                    m.then_inc(X.hg_pv, 1)
                    pe.wait_ge(X.hg_sq, u + 1)
                    token_sums(lambda k: ho_sq[:, :], 1, bank[7]).then_inc(X.hg_st, 1)
                    pe.wait_ge(X.hg_rc, u + 1)
                    spread(bank[7]).then_inc(X.hg_bc, 1)
                A = att["a"]
                phase_start(l, C_P3)
                pe.wait_ge(X.hg_out, l * 4 + 4 + 1)
                pe.nop(nofuse=True)
                with pe.Fori(0, 4) as i:
                    u = l * 4 + i
                    scores(A, u)
                    product(l, C_P3, i, 0, bank[0], lag=2)
                    merge(l, C_P3, i, 1, bank[2], bank[3], yc_hi, yc_lo)
                    pe.wait_ge(A["vtok"], u + 1)
                    for t in range(TT_):
                        pe.wait_ge(A["pd"], u * 4 + (t + 1))
                        if t >= 2:
                            pe.wait_ge(A["pt"], u * 4 + (t - 1))
                        transposes(bank[6 + t % 2], S[:, 0, t, :]).then_inc(A["tr"], 1)
                    product(l, C_P3, i, 2, bank[1], lag=2)
                    pe.wait_ge(A["pt"], u * 4 + 4)
                    for k in range(TT_):
                        m = mm(bank[4][:, :], v_tok[:, k * P:(k + 1) * P], pT_a[:, k, :],
                               start=(k == 0), stop=(k == TT_ - 1))
                    m.then_inc(A["pv"], 1)
                    merge(l, C_P3, i, 3, bank[2], bank[3], yc_hi, yc_lo)
                    pe.wait_ge(A["osq"], u + 1)
                    token_sums(lambda k: o_sq[:, :], 1, bank[5]).then_inc(A["st"], 1)
                    pe.wait_ge(A["rc"], u + 1)
                    spread(bank[7]).then_inc(A["bc"], 1)
                B = att["b"]
                phase_start(l, C_P4)
                pe.wait_ge(A["out"], l * 4 + 4 + 1)
                pe.nop(nofuse=True)
                with pe.Fori(0, 2) as i:
                    for r in range(2):
                        u = l * 4 + i * 2 + r
                        scores(B, u)
                        merge(l, C_P4, i, 2 * r, bank[0], bank[1], ya_hi, ya_lo)
                        pe.wait_ge(B["vtok"], u + 1)
                        for g in range(8):
                            pe.wait_ge(B["pd"], u * 8 + (g + 1))
                            if g >= 2:
                                pe.wait_ge(B["pt"], u * 8 + (g - 1))
                            transposes(bank[6 + g % 2], S[:, g // 4, g % 4, :]).then_inc(B["tr"], 1)
                        for m_ in range(2):
                            pe.wait_ge(B["pt"], u * 8 + 4 * (m_ + 1))
                            for k in range(TT_):
                                m = mm(bank[4][64 * m_:64 * m_ + 64, :],
                                       v_tok[:, k * P + 64 * m_:k * P + 64 * m_ + 64], pT_b[:, m_, k, :],
                                       start=(k == 0), stop=(k == TT_ - 1))
                        m.then_inc(B["pv"], 1)
                        merge(l, C_P4, i, 2 * r + 1, bank[2], bank[3], ya_hi, ya_lo)
                phase_start(l, C_P5)
                pe.wait_ge(B["out"], l * 4 + 4 + 1)
                pe.nop(nofuse=True)
                with pe.Fori(0, 2) as i:
                    for c in range(4):
                        merge(l, C_P5, i, c, bank[2 * (c % 2)], bank[2 * (c % 2) + 1], yb_hi, yb_lo)
                phase_start(l, C_P6)
                pe.wait_ge(X.m_ready, l + 1)
                pe.nop(nofuse=True)
                with pe.Fori(0, 2) as i:
                    for c in range(4):
                        weights(l, C_P6, i, c, 4)
                        block_products(bank[c], c, [(k, k) for k in range(KD)], lambda k: m_hi[:, k, :],
                                       lambda k: m_lo[:, k, :], True, True).then_inc(X.chunk_done, 1)
                norm(l * 3 + 2)
                ffn(l, 1)
            norm(DEPTH * 3)

        @block.scalar
        def _(act):
            A_ = nc.scalar.activation
            act.dma_start(ident[:, :], ident_c[:, :]).then_inc(X.const_in, 16)
            act.dma_start(mask_f[:, :, :], masks_c.rearrange("p (j n) -> p j n", n=P)).then_inc(X.const_in, 16)
            act.dma_start(par2[:, :].rearrange("p (l c) -> p l c", l=DEPTH)[:, :, 0:26], gains[:, :, :])\
                .then_inc(X.par_in, 16)
            act.dma_start(lbr, lb_raw[:, :]).then_inc(X.par_in, 16)
            act.dma_start(lamp[0:64, 0:8], lam_in[:, :]).then_inc(X.par_in, 16)
            act.wait_ge(X.pre_exp, 1)
            act.wait_ge(X.pre_lam, 2)
            A_(lamp[:, 12:16], bank[7][:, 0:4], ACT.Exp)
            A_(lbt[:, 0:8], lbr, ACT.Exp)
            act.drain().then_inc(X.pre_exp, 1)

            def norm(nu):
                for k in range(KD):
                    act.wait_ge(X.h_upd, nu * KD + (k + 1))
                    A_(h_sq[:, k, :], h[:, k, :], ACT.Square).then_inc(X.sq_ready, 1)
                act.wait_ge(X.n_ms, nu + 1)
                A_(rt, ms, ACT.Sqrt).then_inc(X.n_rt, 1)

            def halves(nx):
                for k in range(KD):
                    act.wait_ge(X.xf_ready, nx * KD + (k + 1))
                    A_(x_hi[:, k, :], x_f[:, k % 2, :], ACT.Copy).then_inc(X.xhi_ready, 1)

            def ffn(l, s):
                with act.Fori(0, KF // 2) as i:
                    for v in range(2):
                        n = l * CH + (GU[s] + 2 * v) + i * 4
                        act.wait_ge(X.chunk_done, n + 3)
                        act.wait_ge(X.prod_taken, n + 2)
                        A_(silu_g[:, v, :], bank[2 * v][:, :], ACT.Silu).then_inc(X.silu_done, 1)

            def take(l, base, i, c, slot):
                n = l * CH + (base + c) + i * 4
                act.wait_ge(X.chunk_done, n + 3)
                act.nop(nofuse=True)
                A_(z[:, bass.ds(slot, 1), :].rearrange("p a n -> p (a n)"), bank[c][:, :], ACT.Copy)\
                    .then_inc(X.prod_taken, 1)

            def gate(l, base, i, c, b, count):
                n = l * CH + (base + c) + i * 4
                act.wait_ge(X.chunk_done, n + 3)
                act.wait_ge(X.gate_done, count + 1)
                A_(gate_t[:, :], bank[b][:, :], ACT.Tanh, scale=0.5).then_inc(X.gate_ready, 1)

            def stage(dst, slot):
                return A_(dst[:, :], z[:, bass.ds(slot, 1), :].rearrange("p a n -> p (a n)"), ACT.Copy)

            def attention_in(a, u, tables, qkv):
                act.wait_ge(a["ttr"], u * 8 + 1)
                for m, row in enumerate(tables):
                    act.dma_start(bias[:, m, :], bias_c[bass.ds(row, 1), :, :].rearrange("a p n -> (a p) n"))\
                        .then_inc(a["tbl"], 16)
                act.wait_ge(a["sc"], u * 8 + 1)
                act.nop(nofuse=True)
                for dst, slot in zip((q_st, k_st, v_st), qkv):
                    stage(dst, slot)
                act.drain().then_inc(a["stage"], 1)
                act.wait_ge(a["vt"], u + 1)
                A_(v_tok[:, :], bank[6][:, :], ACT.Copy).then_inc(a["vtok"], 1)
                for g in range(8):
                    act.wait_ge(a["ttr"], u * 8 + (g + 1) + 1)
                    A_(S[:, g // 4, g % 4, :], S[:, g // 4, g % 4, :], ACT.Exp, bias=neg_max[:, g:g + 1],
                       scale=-1.0, accum_out=p_sum[:, g:g + 1]).then_inc(a["exp"], 1)

            def p_columns(a, u, n, g, dst):
                t = g % 4
                act.wait_ge(a["tr"], u * n + (g + 1))
                A_(dst[:, :, t * P:(t + 1) * P], bank[6 + g % 2][:, :].rearrange("p (k n) -> p k n", n=P),
                   ACT.Copy).then_inc(a["pt"], 1)

            with act.Fori(0, DEPTH) as l:
                norm(l * 3)
                halves(l * 3)
                ffn(l, 0)
                norm(l * 3 + 1)
                halves(l * 3 + 1)
                act.wait_ge(X.xn_ready, l * 24 + 16)
                act.dma_start(h_save.rearrange("(k p) n -> p k n", p=P), h[:, :, :]).then_inc(X.h_saved, 16)
                with act.Fori(0, 5) as i:
                    for c in range(4):
                        take(l, C_P1, i, c, i * 4 + c)
                with act.Fori(0, 4) as i:
                    u = l * 4 + i
                    act.wait_ge(X.prod_taken, l * CH + (C_P2 + 4))
                    act.wait_ge(X.lv_mul, u * 6 + 1)
                    act.nop(nofuse=True)
                    stage(hq, i + 8)
                    stage(hi_st, i + 12)
                    act.drain().then_inc(X.hg_stage, 1)
                    act.wait_ge(X.hg_nf, u + 1)
                    A_(kk[:, :, :], nf[:, :, :], ACT.Exp)
                    act.drain()
                    A_(ln1[:, :, :], kk[:, :, :], ACT.Ln, bias=1.0)
                    A_(gg[:, :, :], kk[:, :, :], ACT.Ln, bias=1.0, scale=lb_h[:, 0:1])
                    act.drain().then_inc(X.hg_ln, 1)
                    act.wait_ge(X.hg_it, u + 1)
                    A_(i_tok[:, :], bank[6][:, :], ACT.Copy).then_inc(X.hg_itok, 1)
                    act.wait_ge(X.hg_ar, u + 1)
                    A_(kk[:, :, :], nf[:, :, :], ACT.Exp).then_inc(X.hg_kexp, 1)
                    take(l, C_P2, i, 0, i + 20)
                    act.wait_ge(X.hg_rem, u + 1)
                    A_(qk64[:, 0:2, :], run[:, :, :], ACT.Exp)
                    A_(qk64[:, 2:4, :], qk64[:, 2:4, :], ACT.Exp)
                    act.drain().then_inc(X.hg_e, 1)
                    take(l, C_P2, i, 1, i + 24)
                    take(l, C_P2, i, 2, i + 28)
                    act.wait_ge(X.hg_out, u + 1)
                    act.nop(nofuse=True)
                    A_(og_t[:, :], z[:, bass.ds(i + 16, 1), :].rearrange("p a n -> p (a n)"), ACT.Tanh, scale=0.5)\
                        .then_inc(X.hg_og, 1)

                    def lv(j):
                        act.wait_ge(X.lv_sub, u * 6 + (j + 1))
                        A_(xy[j % 2][:, :, :], xy[j % 2][:, :, :], ACT.Exp).then_inc(X.lv_exp, 1)

                    lv(0)
                    lv(1)
                    for a in range(4):
                        act.wait_ge(X.od_mm, u * 4 + (a + 1))
                        for lo_, hi_ in ((0, a), (a + 1, 4)):
                            if hi_ > lo_:
                                A_(AT[:, a, lo_ * P:hi_ * P], bank[6 + a % 2][:, lo_ * P:hi_ * P], ACT.Copy)
                        act.drain().then_inc(X.od_taken, 1)
                    lv(2)
                    lv(3)
                    take(l, C_P2, i, 3, i + 32)
                    lv(4)
                    lv(5)
                    act.wait_ge(X.hg_pv, u + 1)
                    A_(ho_sq[:, :], bank[6][:, :], ACT.Square)
                    A_(ho_f[:, :], bank[6][:, :], ACT.Copy)
                    act.drain().then_inc(X.hg_sq, 1)
                    act.wait_ge(X.hg_ms, u + 1)
                    A_(rt, ms, ACT.Sqrt).then_inc(X.hg_rt, 1)
                A = att["a"]
                act.wait_ge(X.hg_out, l * 4 + 4 + 1)
                act.wait_ge(X.prod_taken, l * CH + (C_P3 + 4))
                act.nop(nofuse=True)
                with act.Fori(0, 4) as i:
                    u = l * 4 + i
                    attention_in(A, u, [i], (i + 20, i + 24, i + 28))
                    gate(l, C_P3, i, 1, 2, l * 24 + i * 2)
                    act.wait_ge(A["pd"], u * 4 + 4)
                    for t in range(TT_):
                        p_columns(A, u, 4, t, pT_a)
                    act.wait_ge(A["pv"], u + 1)
                    A_(o_sq[:, :], bank[4][:, :], ACT.Square)
                    A_(o_f[:, :], bank[4][:, :], ACT.Copy)
                    act.drain().then_inc(A["osq"], 1)
                    gate(l, C_P3, i, 3, 2, l * 24 + i * 2 + 1)
                    act.wait_ge(A["ms"], u + 1)
                    A_(rt, ms, ACT.Sqrt).then_inc(A["rt"], 1)
                B = att["b"]
                act.wait_ge(A["out"], l * 4 + 4 + 1)
                act.wait_ge(X.prod_taken, l * CH + (C_P4 + 4))
                act.nop(nofuse=True)
                with act.Fori(0, 2) as i:
                    for r in range(2):
                        u = l * 4 + i * 2 + r
                        p = i * 2 + r
                        attention_in(B, u, [i * 4 + (4 + 2 * r), i * 4 + (5 + 2 * r)],
                                     (p + 32, p + 36, p + 40))
                        gate(l, C_P4, i, 2 * r, 0, l * 24 + i * 4 + (8 + 2 * r))
                        for g in range(8):
                            p_columns(B, u, 8, g, pT_b[:, g // 4, :, :])
                        gate(l, C_P4, i, 2 * r + 1, 2, l * 24 + i * 4 + (9 + 2 * r))
                act.wait_ge(B["out"], l * 4 + 4 + 1)
                act.wait_ge(X.h_saved, l * 16 + 16)
                act.dma_start(h[:, :, :], h_save.rearrange("(k p) n -> p k n", p=P)).then_inc(X.h_back, 16)
                with act.Fori(0, 2) as i:
                    for c in range(4):
                        gate(l, C_P5, i, c, 2 * (c % 2), l * 24 + i * 4 + (16 + c))
                norm(l * 3 + 2)
                halves(l * 3 + 2)
                ffn(l, 1)
            norm(DEPTH * 3)

        @block.vector
        def _(dve):
            V = nc.vector
            dve.sem_inc(X.prod_taken, 4)
            dve.sem_inc(X.lev_taken, 2)
            for s in (X.hg_out, X.lv_mul, X.gate_done, att["a"]["ttr"], att["a"]["out"], att["b"]["ttr"], att["b"]["out"]):
                dve.sem_inc(s, 1)
            V.memset(ones[:, :], 1.0)
            V.memset(run_mask[:, :], 1.0)
            dve.wait_ge(X.par_in, 64)
            V.tensor_tensor(lamp[0:64, 8:10], lamp[0:64, 0:2], lamp[0:64, 2:4], ALU.mult)
            V.tensor_tensor(lamp[0:64, 10:12], lamp[0:64, 4:6], lamp[0:64, 6:8], ALU.mult)
            dve.drain().then_inc(X.pre_lam, 1)
            V.memset(run_mask[:, :].rearrange("p (c t) -> p c t", t=CS)[:, :, 0:1], 0.0)
            V.tensor_tensor(lbt[:, 8:12], lbr[:, 0:4], lbr[:, 4:8], ALU.max)
            dve.drain()
            V.tensor_tensor(lbr[:, 0:4], lbr[:, 0:4], lbt[:, 8:12], ALU.subtract)
            V.tensor_tensor(lbr[:, 4:8], lbr[:, 4:8], lbt[:, 8:12], ALU.subtract)
            dve.drain().then_inc(X.pre_lam, 1)
            dve.wait_ge(X.pre_exp, 2)
            V.tensor_tensor(lbt[:, 8:12], lbt[:, 0:4], lbt[:, 4:8], ALU.add)
            V.tensor_tensor(lamp[:, 16:18], lamp[:, 14:16], lamp[:, 12:14], ALU.subtract)
            dve.drain()
            V.reciprocal(lbt[:, 8:12], lbt[:, 8:12])
            dve.drain()
            for l in range(DEPTH):
                p0 = l * NPAR
                lam_init = 0.8 - 0.6 * float(np.exp(-0.3 * l))
                if l == 0:
                    V.memset(par2[:, p0 + LB:p0 + LB + 4], 0.0)
                else:
                    V.tensor_tensor(par2[:, p0 + LB:p0 + LB + 4], lbt[:, 4:8], lbt[:, 8:12], ALU.mult)
                V.tensor_scalar(par2[:, p0 + NLAM:p0 + NLAM + 1], lamp[:, 16 + l:17 + l], -lam_init, None, ALU.add)
                V.tensor_scalar(par2[:, p0 + G_SUB:p0 + G_SUB + 1], par2[:, p0 + G_SUB:p0 + G_SUB + 1],
                                1.0 - lam_init, None, ALU.mult)
                V.tensor_scalar(par2[:, p0 + G_HG:p0 + G_HG + 1], par2[:, p0 + G_HG:p0 + G_HG + 1],
                                0.5, None, ALU.mult)
            dve.drain()
            for l in range(DEPTH):
                p0 = l * NPAR
                V.tensor_scalar(par2[:, p0 + OMLB:p0 + OMLB + 4], par2[:, p0 + LB:p0 + LB + 4],
                                -1.0, 1.0, ALU.mult, ALU.add)
            V.memset(par2[:, NLAM + 1:NLAM + 2], 0.0)
            V.memset(par2[:, NPAR + NLAM + 1:NPAR + NLAM + 2], 0.0)
            dve.drain()
            dve.wait_ge(X.x_in, 16)
            dve.sem_inc(X.h_upd, KD)
            dve.wait_ge(X.const_in, 32)
            V.tensor_copy(masks[:, :, :].rearrange("p j (a n) -> p j a n", n=P),
                          mask_f[:, :, :].rearrange("p j (a n) -> p j a n", a=1)
                          .broadcast_to([P, len(LEVELS), TT_, P]))
            dve.drain()

            def inverse_rms(width, stat, done_ms, rt_in, done_rc, nu, ready):
                dve.wait_ge(ready, nu + 1)
                V.tensor_scalar(ms, stat[:, 0:4], 1.0 / width, EPS, ALU.mult, ALU.add).then_inc(done_ms, 1)
                dve.wait_ge(rt_in, nu + 1)
                V.reciprocal(rs, rt).then_inc(done_rc, 1)

            def norm(nu, g0):
                inverse_rms(D, bank[7], X.n_ms, X.n_rt, X.n_rc, nu, X.n_stat)
                dve.wait_ge(X.n_bc, nu + 1)
                for k in range(KD + 1):
                    if k < KD:
                        V.scalar_tensor_tensor(x_f[:, k % 2, :], h[:, k, :], par[:, g0 + k:g0 + k + 1],
                                               bank[6][:, :], ALU.mult, ALU.mult).then_inc(X.xf_ready, 1)
                    if k >= 1:
                        dve.wait_ge(X.xhi_ready, nu * KD + k)
                        V.tensor_tensor(x_lo[:, k - 1, :], x_f[:, (k - 1) % 2, :],
                                        x_hi[:, k - 1, :].bitcast(F32), ALU.subtract)
                        dve.drain().then_inc(X.xn_ready, 1)

            def ffn(l, s):
                with dve.Fori(0, KF // 2) as i:
                    for v in range(2):
                        n = l * CH + (GU[s] + 2 * v + 1) + i * 4
                        f = i * 2 + v
                        dve.wait_ge(X.chunk_done, n + 3)
                        dve.wait_ge(X.silu_done, l * 44 + i * 2 + (22 * s + v + 1))
                        V.tensor_tensor(act_f[:, v, :], silu_g[:, v, :], bank[2 * v + 1][:, :], ALU.mult)
                        dve.drain().then_inc(X.prod_taken, 2)
                        hi = act_hi[:, bass.ds(f, 1), :].rearrange("p a n -> p (a n)")
                        lo = act_lo[:, bass.ds(f, 1), :].rearrange("p a n -> p (a n)")
                        V.tensor_copy(hi, act_f[:, v, :])
                        dve.drain()
                        V.tensor_tensor(lo, act_f[:, v, :], hi.bitcast(F32), ALU.subtract)
                        dve.drain().then_inc(X.act_ready, 1)
                with dve.Fori(0, KD // 2) as i:
                    for v in range(2):
                        n = l * CH + (DN[s] + 2 * v + 1) + i * 4
                        dve.wait_ge(X.chunk_done, n + 3)
                        hj = h[:, bass.ds(i * 2 + v, 1), :].rearrange("p a n -> p (a n)")
                        V.scalar_tensor_tensor(hj, bank[2 * v][:, :], 0.5, hj, ALU.mult, ALU.add)\
                            .then_inc(X.h_upd, 1)
                        dve.drain().then_inc(X.prod_taken, 2)

            def take(l, base, i, c, b, slot):
                n = l * CH + (base + c) + i * 4
                dve.wait_ge(X.chunk_done, n + 3)
                dve.nop(nofuse=True)
                V.tensor_copy(z[:, bass.ds(slot, 1), :].rearrange("p a n -> p (a n)"), bank[b][:, :])\
                    .then_inc(X.prod_taken, 1)

            def gated_sum(l, base, i, c, b, count, j, how):
                dve.wait_ge(X.gate_ready, count + 1)
                dve.wait_ge(X.chunk_done, l * CH + (base + c + 3) + i * 4)
                mj = merged[:, bass.ds(j, 1), :].rearrange("p a n -> p (a n)")
                dst = mj if how == "first" else gated[:, :]
                V.scalar_tensor_tensor(dst, gate_t[:, :], 1.0, bank[b][:, :], ALU.add, ALU.mult)
                dve.drain().then_inc(X.prod_taken, 1)
                if how == "first":
                    dve.sem_inc(X.gate_done, 1)
                    return
                V.tensor_tensor(mj if how == "more" else gated[:, :], gated[:, :], mj, ALU.add)
                dve.drain().then_inc(X.gate_done, 1)
                if how == "last":
                    mh = m_hi[:, bass.ds(j, 1), :].rearrange("p a n -> p (a n)")
                    ml = m_lo[:, bass.ds(j, 1), :].rearrange("p a n -> p (a n)")
                    V.tensor_scalar(mh, gated[:, :], 0.5, None, ALU.mult)
                    dve.drain()
                    V.scalar_tensor_tensor(ml, gated[:, :], 0.5, mh.bitcast(F32), ALU.mult, ALU.subtract)
                    dve.drain()

            def row_max(a, u, tables):
                dve.wait_ge(a["tbl"], (u + 1) * (16 * tables))
                for g in range(8):
                    m, t = divmod(g, 4)
                    dve.wait_ge(a["sc"], u * 8 + (g + 1) + 1)
                    dve.nop(nofuse=True)
                    V.tensor_tensor_reduce(out=S[:, m, t, :], in0=bank[4 + g % 2][:, :],
                                           in1=bias[:, m if tables == 2 else 0, 384 - t * P:384 - t * P + SEQ],
                                           scale=-SCALE, scalar=3.0e38, op0=ALU.add, op1=ALU.min,
                                           accum_out=neg_max[:, g:g + 1])
                    dve.drain().then_inc(a["ttr"], 1)
                dve.wait_ge(a["exp"], u * 8 + 8)
                V.reciprocal(p_rs, p_sum)
                dve.drain()

            def split(hi, lo, src):
                V.tensor_copy(hi, src)
                dve.drain()
                V.tensor_tensor(lo, src, hi.bitcast(F32), ALU.subtract)

            tile_of = lambda t, j: t[:, bass.ds(j, 1), :].rearrange("p a n -> p (a n)")

            with dve.Fori(0, DEPTH) as l:
                V.tensor_copy(par, par2[:, bass.ds(l * NPAR, NPAR)])
                dve.drain()
                norm(l * 3, G_FFN1)
                ffn(l, 0)
                norm(l * 3 + 1, G_MIX)
                dve.wait_ge(X.prod_taken, l * CH + (C_P2 + 4))
                dve.wait_ge(X.h_saved, l * 16 + 16)
                dve.nop(nofuse=True)
                with dve.Fori(0, 4) as i:
                    u = l * 4 + i
                    f2 = z[:, 0:8, :].rearrange("p (d a) n -> p d a n", d=2)[:, :, bass.ds(i, 1), :]\
                        .rearrange("p d a n -> p d (a n)")
                    V.tensor_copy(lb_h[:, 0:1], par[:, bass.ds(i + LB, 1)])
                    V.tensor_copy(lb_h[:, 1:2], par[:, bass.ds(i + OMLB, 1)])
                    V.tensor_scalar(nf[:, :, :], f2, -1.0, F_CAP, ALU.mult, ALU.min)
                    dve.drain().then_inc(X.hg_nf, 1)
                    dve.wait_ge(X.hg_ln, u + 1)
                    V.tensor_tensor(nf[:, :, :], nf[:, :, :], ln1[:, :, :], ALU.subtract)
                    V.tensor_tensor(gg[:, :, :], gg[:, :, :], ln1[:, :, :], ALU.subtract)
                    dve.drain().then_inc(X.hg_ar, 1)
                    V.tensor_tensor_scan(run[:, 0, :], run_mask[:, :], gg[:, 0, :], 0.0, ALU.mult, ALU.add)
                    V.tensor_tensor_scan(run[:, 1, ::-1], run_mask[:, :], gg[:, 1, ::-1], 0.0, ALU.mult, ALU.add)
                    dve.drain()
                    rc = lambda t: t.rearrange("p (c t) -> p c t", t=CS)
                    V.tensor_tensor(rc(qk64[:, 2, :]), rc(run[:, 0, :])[:, :, CS - 1:CS].broadcast_to([P, NC, CS]),
                                    rc(run[:, 0, :]), ALU.subtract)
                    V.tensor_tensor(rc(qk64[:, 3, :]), rc(run[:, 1, :])[:, :, 0:1].broadcast_to([P, NC, CS]),
                                    rc(run[:, 1, :]), ALU.subtract)
                    dve.drain().then_inc(X.hg_rem, 1)
                    dve.wait_ge(X.hg_kexp, u + 1)
                    V.tensor_scalar(kk[:, :, :], kk[:, :, :], lb_h[:, 1:2], None, ALU.mult)
                    dve.drain()
                    V.tensor_tensor(k_sum[:, :], kk[:, 0, :], kk[:, 1, :], ALU.add)
                    dve.drain().then_inc(X.hg_ks, 1)

                    def halves_of(t, m):
                        return t.rearrange("p (b s m) -> p b s m", s=2, m=m)

                    def level_sub(j):
                        m = LEVELS[j]
                        nb = SEQ // (2 * m)
                        x, y = halves_of(xy[j % 2][:, 0, :], m), halves_of(xy[j % 2][:, 1, :], m)
                        rf, rb = halves_of(run[:, 0, :], m), halves_of(run[:, 1, :], m)
                        cf = rf[:, :, 0, m - 1:m].broadcast_to([P, nb, m])
                        cb = rb[:, :, 1, 0:1].broadcast_to([P, nb, m])
                        V.tensor_tensor(x[:, :, 1, :], rf[:, :, 1, :], cf, ALU.subtract)
                        V.tensor_tensor(y[:, :, 0, :], cf, rf[:, :, 0, :], ALU.subtract)
                        V.tensor_tensor(x[:, :, 0, :], rb[:, :, 0, :], cb, ALU.subtract)
                        V.tensor_tensor(y[:, :, 1, :], cb, rb[:, :, 1, :], ALU.subtract)
                        dve.drain().then_inc(X.lv_sub, 1)

                    def level_mul(j):
                        m = LEVELS[j]
                        dve.wait_ge(X.lv_exp, u * 6 + (j + 1))
                        dve.wait_ge(X.lev_mm, u * 8 + (j + 2 if j >= 2 else 1 + j))
                        e, o = xy[j % 2], qkl[j % 2]
                        dve.wait_ge(X.hg_stage, u + 1)
                        V.tensor_tensor(o[:, 0, :], e[:, 0, :], hq[:, :], ALU.mult)
                        for s in range(2):
                            V.tensor_tensor(halves_of(o[:, 1, :], m)[:, :, s, :], halves_of(e[:, 1, :], m)[:, :, s, :],
                                            halves_of(kk[:, s, :], m)[:, :, s, :], ALU.mult)
                        dve.drain().then_inc(X.lv_mul, 1)

                    def level_take(j):
                        dve.wait_ge(X.lev_mm, u * 8 + (j + 3))
                        dve.nop(nofuse=True)
                        V.copy_predicated(ATd, masks[:, j, :].rearrange("p (a n) -> p a n", n=P),
                                          bank[4 + j % 2][:, :].rearrange("p (a n) -> p a n", n=P))
                        dve.drain().then_inc(X.lev_taken, 1)

                    level_sub(0)
                    level_sub(1)
                    dve.wait_ge(X.hg_e, u + 1)
                    V.tensor_copy(tot[:, 0:8], rc(qk64[:, 0, :])[:, :, CS - 1])
                    V.tensor_copy(tot[:, 8:16], rc(qk64[:, 1, :])[:, :, 0])
                    dve.drain()
                    V.tensor_tensor(qk64[:, 0:2, :], qk64[:, 0:2, :],
                                    hq[:, :].rearrange("p (a n) -> p a n", a=1).broadcast_to([P, 2, SEQ]), ALU.mult)
                    V.tensor_tensor(qk64[:, 2:4, :], qk64[:, 2:4, :], kk[:, :, :], ALU.mult)
                    tv = tot.rearrange("p (a s) -> p a s", s=2)
                    V.tensor_tensor(ttot, tv[:, :, 0], tv[:, :, 1], ALU.mult)
                    dve.drain().then_inc(X.hg_q64, 1)
                    dve.wait_ge(X.lev_mm, u * 8 + 1)
                    V.tensor_copy(ATd, bank[4][:, :].rearrange("p (a n) -> p a n", n=P))
                    dve.drain().then_inc(X.lev_taken, 1)
                    dve.wait_ge(X.lev_mm, u * 8 + 2)
                    b5 = bank[5][:, :].rearrange("p (a n) -> p a n", n=P)
                    V.tensor_copy(ATd[0:CS, :, CS:P], b5[0:CS, :, CS:P])
                    V.tensor_copy(ATd[CS:P, :, 0:CS], b5[CS:P, :, 0:CS])
                    dve.drain().then_inc(X.lev_taken, 1)
                    r4 = lambda t: t.rearrange("p (a s n) -> p a s n", s=2, n=CS)
                    for row, outer, d in ((0, 1, 0), (2, 0, 0), (1, 0, 1), (3, 1, 1)):
                        t_in = tot[:, 8 * d:8 * d + 8].rearrange("p (a s) -> p a s", s=2)[:, :, 1 - outer:2 - outer]
                        v = r4(qk64[:, row, :])[:, :, outer, :]
                        V.tensor_tensor(v, v, t_in.broadcast_to([P, TT_, CS]), ALU.mult)
                    dve.drain()
                    sl = lambda t: slice(t * P, (t + 1) * P)
                    sc = lambda d, t: ttot[:, 4 * d + t:4 * d + t + 1]
                    V.tensor_scalar(q_far[:, 0, :], qk64[:, 0, sl(2)], sc(0, 1), None, ALU.mult)
                    V.tensor_scalar(q_far[:, 1, :], qk64[:, 0, sl(3)], sc(0, 2), None, ALU.mult)
                    V.tensor_scalar(q_far[:, 3, :], qk64[:, 1, sl(1)], sc(1, 2), None, ALU.mult)
                    V.tensor_scalar(q_far[:, 4, :], qk64[:, 1, sl(0)], sc(1, 1), None, ALU.mult)
                    dve.drain()
                    V.tensor_scalar(q_far[:, 2, :], q_far[:, 1, :], sc(0, 1), None, ALU.mult)
                    V.tensor_scalar(q_far[:, 5, :], q_far[:, 4, :], sc(1, 2), None, ALU.mult)
                    dve.drain().then_inc(X.hg_q128, 1)
                    for j in range(len(LEVELS)):
                        level_mul(j)
                        if j + 2 < len(LEVELS):
                            level_sub(j + 2)
                        if j >= 1:
                            level_take(j - 1)
                    level_take(len(LEVELS) - 1)
                    dve.wait_ge(X.hg_og, u + 1)
                    V.scalar_tensor_tensor(og_t[:, :], og_t[:, :], 1.0, tile_of(z, i + 16), ALU.add, ALU.mult)
                    inverse_rms(P, bank[7], X.hg_ms, X.hg_rt, X.hg_rc, u, X.hg_st)
                    dve.wait_ge(X.hg_bc, u + 1)
                    V.scalar_tensor_tensor(ho_f[:, :], ho_f[:, :], par[:, G_HG:G_HG + 1], bank[7][:, :],
                                           ALU.mult, ALU.mult)
                    dve.drain()
                    V.tensor_tensor(ho_f[:, :], ho_f[:, :], og_t[:, :], ALU.mult)
                    dve.drain()
                    split(tile_of(yc_hi, i), tile_of(yc_lo, i), ho_f[:, :])
                    dve.drain().then_inc(X.hg_out, 1)
                A = att["a"]
                with dve.Fori(0, 4) as i:
                    u = l * 4 + i
                    row_max(A, u, 1)
                    V.tensor_scalar(p_c2, p_rs[:, 4:8], par[:, NLAM:NLAM + 1], None, ALU.mult)
                    for t in range(TT_):
                        V.tensor_scalar(S[:, 0, t, :], S[:, 0, t, :], p_rs[:, t:t + 1], None, ALU.mult)
                    dve.drain()
                    for t in range(TT_):
                        V.scalar_tensor_tensor(S[:, 0, t, :], S[:, 1, t, :], p_c2[:, t:t + 1], S[:, 0, t, :],
                                               ALU.mult, ALU.add).then_inc(A["pd"], 1)
                    take(l, C_P3, i, 0, 0, i + 36)
                    gated_sum(l, C_P3, i, 1, 3, l * 24 + i * 2, i * 2, "first")
                    take(l, C_P3, i, 2, 1, i + 40)
                    gated_sum(l, C_P3, i, 3, 3, l * 24 + i * 2 + 1, i * 2 + 1, "first")
                    inverse_rms(P, bank[5], A["ms"], A["rt"], A["rc"], u, A["st"])
                    dve.wait_ge(A["bc"], u + 1)
                    V.scalar_tensor_tensor(o_f[:, :], o_f[:, :], par[:, G_SUB:G_SUB + 1], bank[7][:, :],
                                           ALU.mult, ALU.mult)
                    dve.drain()
                    split(tile_of(ya_hi, i), tile_of(ya_lo, i), o_f[:, :])
                    dve.drain().then_inc(A["out"], 1)
                B = att["b"]
                with dve.Fori(0, 2) as i:
                    for r in range(2):
                        u = l * 4 + i * 2 + r
                        row_max(B, u, 2)
                        for g in range(8):
                            V.tensor_scalar(S[:, g // 4, g % 4, :], S[:, g // 4, g % 4, :], p_rs[:, g:g + 1],
                                            None, ALU.mult).then_inc(B["pd"], 1)
                        gated_sum(l, C_P4, i, 2 * r, 1, l * 24 + i * 4 + (8 + 2 * r), i * 4 + 2 * r, "more")
                        dve.wait_ge(B["pv"], u + 1)
                        split(tile_of(yb_hi, i * 2 + r), tile_of(yb_lo, i * 2 + r), bank[4][:, :])
                        dve.drain().then_inc(B["out"], 1)
                        gated_sum(l, C_P4, i, 2 * r + 1, 3, l * 24 + i * 4 + (9 + 2 * r), i * 4 + 2 * r + 1, "more")
                with dve.Fori(0, 2) as i:
                    for c in range(4):
                        gated_sum(l, C_P5, i, c, 2 * (c % 2) + 1, l * 24 + i * 4 + (16 + c), i * 4 + c, "last")
                dve.drain().then_inc(X.m_ready, 1)
                dve.wait_ge(X.h_back, l * 16 + 16)
                dve.nop(nofuse=True)
                with dve.Fori(0, 2) as i:
                    for c in range(4):
                        dve.wait_ge(X.chunk_done, l * CH + (C_P6 + c + 3) + i * 4)
                        hj = tile_of(h, i * 4 + c)
                        V.tensor_tensor(hj, bank[c][:, :], hj, ALU.add).then_inc(X.h_upd, 1)
                        dve.drain().then_inc(X.prod_taken, 1)
                norm(l * 3 + 2, G_FFN2)
                ffn(l, 1)
            nu = DEPTH * 3
            inverse_rms(D, bank[7], X.n_ms, X.n_rt, X.n_rc, nu, X.n_stat)
            dve.wait_ge(X.n_bc, nu + 1)
            for k in range(KD):
                V.scalar_tensor_tensor(h_sq[:, k, :], h[:, k, :], fin_g[:, k:k + 1], bank[6][:, :],
                                       ALU.mult, ALU.mult).then_inc(X.out_ready, 1)


def alibi_tables():
    n = 12
    slopes = np.exp2(np.float32(-8.0) * np.arange(1, n + 1, dtype=np.float32) / np.float32(n)).astype(np.float32)
    d = np.arange(UW)[None, :] - 384 - np.arange(P)[:, None]
    dist = np.abs(d)
    count = np.zeros(d.shape, np.int64)
    for window, dilation in ((128, 1), (512, 4), (2048, 16)):
        count += (dist % dilation == 0) & (dist // dilation <= window // (2 * dilation))
    ln_count = np.where(count > 0, np.log(np.maximum(count, 1)), -1e30)
    out = np.zeros((n, P, UW), np.float32)
    for row, s in enumerate((0, 3, 6, 9, 1, 2, 4, 5, 7, 8, 10, 11)):
        b = (-slopes[s] * dist.astype(np.float32)).astype(np.float64)
        out[row] = ((b + (ln_count if row >= 4 else 0)) / SCALE).astype(np.float32)
    return out


def level_masks():
    s, t = np.arange(P)[:, None], np.arange(P)[None, :]
    rows = [((s // (2 * m) == t // (2 * m)) & (s // m != t // m)) for m in LEVELS]
    return np.concatenate(rows, axis=1).astype(np.float32)


def kernel(**inputs):
    import concourse.bacc as bacc
    from concourse.bass_utils import run_bass_kernel_spmd

    a = {k: np.asarray(v) for k, v in inputs.items()}

    def blocks(w, cols):
        k, n = w.shape
        b = w.reshape(k // P, P, n // P, P).transpose(2, 1, 0, 3)
        return b[cols]

    def chunks(w, cols):
        b = blocks(w, cols)
        return b.reshape(b.shape[0], P, -1)

    gu, dn, proj, mrg, wo = [], [], [], [], []
    order = list(range(28, 32)) + list(range(32, 36)) + list(range(24, 28)) + list(range(36, 40)) + list(range(40, 44))
    for i in range(4):
        order += [i, 4 + i, 8 + i, 12 + i]
    for i in range(4):
        order += [16 + i, 20 + i]
    for l in range(DEPTH):
        for f in ("ffn1", "ffn2"):
            g = chunks(a[f + "_w_gate"][l], slice(None))
            u = chunks(a[f + "_w_up"][l], slice(None))
            gu.append(np.stack([g, u], axis=1).reshape(-1, P, D))
            d = blocks(a[f + "_w_down"][l], slice(None)).reshape(KD, P, 2, HALF * P).transpose(0, 2, 1, 3)
            dn.append(d.reshape(-1, P, HALF * P))
        proj.append(chunks(a["w_in"][l], order))
        gates = chunks(a["w_in"][l], slice(44, 68)).reshape(3, KD, P, D)
        for b, name in ((2, "w_branch_c"), (0, "w_branch_a"), (1, "w_branch_b")):
            mrg.append(np.concatenate([gates[b], chunks(a[name][l], slice(None))], axis=2))
        wo.append(chunks(a["w_out"][l], slice(None)))
    per_p = lambda v: v.reshape(DEPTH, -1, P).transpose(2, 0, 1)
    gains = np.concatenate([per_p(a[n]) for n in ("ffn1_norm", "mix_norm", "ffn2_norm", "diff_subln", "hgrn_norm")],
                           axis=2)
    lam_in = np.concatenate([a["diff_lambda_" + n].T for n in ("q1", "k1", "q2", "k2")], axis=1)
    arrays = {
        "xT": a["x"][0].T, "wgu": np.concatenate(gu), "wdn": np.concatenate(dn),
        "wproj": np.concatenate(proj), "wmerge": np.concatenate(mrg), "wout": np.concatenate(wo),
        "gains": gains, "final_g": a["final_norm"].reshape(KD, P).T,
        "lb_raw": per_p(a["hgrn_lower_bounds"]).reshape(P, -1), "lam_in": lam_in,
        "ident": np.eye(P, dtype=np.float32), "masks": level_masks(), "bias": alibi_tables(),
    }
    arrays = {k: np.ascontiguousarray(v) for k, v in arrays.items()}

    nc = bacc.Bacc("TRN2", target_bir_lowering=False, num_devices=1, dynamic_dma_scratch_size=1024)
    aps = [nc.dram_tensor("in_" + k, v.shape, mybir.dt.from_np(v.dtype), kind="ExternalInput").ap()
           for k, v in arrays.items()]
    h_save = nc.dram_tensor("h_save", (D, SEQ), F32, kind="Internal").ap()
    out = nc.dram_tensor("out_T", (D, SEQ), F32, kind="ExternalOutput").ap()
    build(nc, *aps, h_save, out)
    r = run_bass_kernel_spmd(nc, [{"in_" + k: v for k, v in arrays.items()}], core_ids=[0])
    return np.ascontiguousarray(r.results[0]["out_T"].T)[None]
```

```python
import concourse.bass as bass
from concourse import mybir
import numpy as np

F32 = mybir.dt.float32
F32R = mybir.dt.float32r
U8 = mybir.dt.uint8
BF16 = mybir.dt.bfloat16
ALU = mybir.AluOpType
ACT = mybir.ActivationFunctionType
AX = mybir.AxisListType

DEPTH, D, SEQ, DFF = 2, 1024, 512, 2816
P = 128
KD = D // P
KF = DFF // P
TT_ = SEQ // P
HALF = KF // 2
BRK = 512 // P
MB = KD + BRK
SLOT = MB * P
EPS = 1e-6
CS = 64
NC = SEQ // CS
LEVELS = (32, 16, 8, 4, 2, 1)
F_CAP = 43.6
SCALE = 64 ** -0.5
BASE = 1152
UW = 896

GU = (0, 136)
DN = (44, 180)
C_P1 = 60
C_P2 = 64
C_P3 = 96
C_P4 = 112
C_P5 = 120
C_P6 = 128
CH = 196

G_FFN1, G_MIX, G_FFN2, G_SUB, G_HG, LB, OMLB, NLAM, NPAR = 0, 8, 16, 24, 25, 26, 30, 34, 36


def build(nc, xT, wgu, wdn, wproj, wmerge, wout, gains, final_g, lb_raw, lam_in, ident_c, masks_c,
          bias_c, h_save, out):
    from contextlib import ExitStack
    ctx = ExitStack()
    with ctx:
        def at(name, words, offset, dt=F32):
            return nc.alloc_sbuf_tensor_at(name, [P, words], dt, offset=BASE + offset)

        def tiles(t, n=SEQ):
            return t[:, :].rearrange("p (a n) -> p a n", n=n)

        KB = 1024
        raw = tiles(at("raw", 4 * SLOT, 0), SLOT)
        w_hi = tiles(at("w_hi", 2 * SLOT, 24 * KB, F32R), SLOT)
        w_lo = tiles(at("w_lo", 2 * SLOT, 36 * KB, F32R), SLOT)
        x_hi = tiles(at("x_hi", KD * SEQ, 48 * KB, F32R))
        x_lo = tiles(at("x_lo", KD * SEQ, 64 * KB, F32R))
        HB = 80 * KB
        h = tiles(at("h", KD * SEQ, HB))
        ZB = 96 * KB
        zs = lambda s: ZB + 2 * KB * s
        z = tiles(at("z", 52 * SEQ, ZB))
        CB = zs(52)
        SB = CB + 6 * KB
        mask_f = tiles(at("mask_f", len(LEVELS) * P, zs(40)), P)
        act_hi = tiles(at("act_hi", KF * SEQ, zs(0), F32R))
        act_lo = tiles(at("act_lo", KF * SEQ, zs(22), F32R))
        silu_g = tiles(at("silu_g", 2 * SEQ, zs(44)))
        act_f = tiles(at("act_f", 2 * SEQ, zs(46)))
        x_f = tiles(at("x_f", 2 * SEQ, zs(48)))
        h_out = tiles(at("h_out", KD * SEQ, SB))
        h_sq = tiles(at("h_sq", 2 * SEQ, SB + 10 * KB))
        sq_sum = at("sq_sum", SEQ, SB + 14 * KB)
        ya_hi = tiles(at("ya_hi", 4 * SEQ, zs(0), F32R))
        ya_lo = tiles(at("ya_lo", 4 * SEQ, zs(5), F32R))
        yc_hi = tiles(at("yc_hi", 4 * SEQ, zs(10), F32R))
        yc_lo = tiles(at("yc_lo", 4 * SEQ, zs(15), F32R))
        yb_hi = tiles(at("yb_hi", 4 * SEQ, zs(24), F32R))
        yb_lo = tiles(at("yb_lo", 4 * SEQ, zs(28), F32R))
        merged = tiles(at("merged", KD * SEQ, zs(44)))
        m_hi = tiles(at("m_hi", KD * SEQ, zs(32), F32R))
        m_lo = tiles(at("m_lo", KD * SEQ, zs(0), F32R))
        o_f = at("o_f", SEQ, zs(20))
        o_sq = at("o_sq", SEQ, zs(21))
        gate_t = at("gate_t", SEQ, zs(22))
        gated = at("gated", SEQ, zs(23))
        S = at("S", 8 * SEQ, HB)[:, :].rearrange("p (m t n) -> p m t n", m=2, n=SEQ)
        pT_a = tiles(at("pT_a", 4 * SEQ, HB + 8 * KB))
        pT_b = [tiles(at(f"pT_b{m}", 4 * SEQ, zs(10 + 5 * m))) for m in range(2)]
        bias = tiles(at("bias", 2 * UW, SB), UW)
        q_st = at("q_st", SEQ, SB + 7 * KB)
        k_st = at("k_st", SEQ, SB + 9 * KB)
        v_st = at("v_st", SEQ, SB + 11 * KB)
        v_tok = at("v_tok", SEQ, SB + 13 * KB)
        nf = tiles(at("nf", 2 * SEQ, HB))
        kk = tiles(at("kk", 2 * SEQ, HB + 4 * KB))
        ln1 = tiles(at("ln1", 2 * SEQ, HB + 8 * KB))
        gg = tiles(at("gg", 2 * SEQ, HB + 12 * KB))
        xy = [nf, ln1]
        run = tiles(at("run", 2 * SEQ, zs(36)))
        qk64 = tiles(at("qk64", 4 * SEQ, zs(38)))
        k_sum = at("k_sum", SEQ, zs(42))
        og_t = at("og_t", SEQ, zs(43))
        qkl = [tiles(at(f"qkl{b}", 2 * SEQ, zs(44 + 2 * b))) for b in range(2)]
        q_far = tiles(at("q_far", 6 * P, zs(48)), P)
        hq = at("hq", SEQ, zs(50))
        hi_st = at("hi_st", SEQ, zs(51))
        AT_ = at("AT", 5 * SEQ, SB)
        AT = tiles(AT_)
        ATd = tiles(AT_, SEQ + P)[:, :, 0:P]
        i_tok = at("i_tok", SEQ, SB + 10 * KB)
        ho_f = at("ho_f", SEQ, SB + 12 * KB)
        ho_sq = at("ho_sq", SEQ, SB + 14 * KB)
        ident = at("ident", P, CB)
        ones = at("ones", P, CB + 512)
        masks = tiles(at("masks", len(LEVELS) * SEQ, CB + 1 * KB, U8))
        run_mask = at("run_mask", SEQ, CB + 4 * KB, BF16)
        par2 = at("par2", DEPTH * NPAR, CB + 5 * KB)
        small = at("small", 160, CB + 5 * KB + 320)
        par = small[:, 0:36]
        ms, rt, rs = small[:, 36:40], small[:, 40:44], small[:, 44:48]
        neg_max, p_sum, p_rs, p_c2 = small[:, 48:56], small[:, 56:64], small[:, 64:72], small[:, 72:76]
        lb_h = small[:, 76:78]
        warm = small[:, 78:79]
        tot, ttot = small[:, 80:96], small[:, 96:104]
        fin_g = small[:, 104:112]
        lbr, lbt, lamp = small[:, 112:120], small[:, 120:132], small[:, 132:152]

        bank = [ctx.enter_context(nc.psum_tensor(f"bank{b}", [P, SEQ], F32)) for b in range(8)]

        names = """par_in sq_added const_in lo_done chunk_done prod_taken silu_done act_ready h_upd
            sq_ready n_stat n_ms n_rt n_rc n_bc xf_ready xhi_ready xn_ready h_saved h_back out_done
            pre_lam pre_exp par_ready gate_done
            hg_stage hg_it hg_itok hg_nf hg_ln hg_ar hg_kexp hg_rem hg_e hg_q64 hg_q128
            hg_og lv_sub lv_exp lv_mul lev_mm lev_taken od_mm od_taken hg_pv hg_sq hg_st hg_ms
            hg_rt hg_rc hg_bc hg_out out_ready gate_ready m_ready""".split()
        sem = {n: ctx.enter_context(nc.semaphore(n)) for n in names}
        x_in = [ctx.enter_context(nc.semaphore(f"x_in{q}")) for q in range(4)]
        raw_in = [ctx.enter_context(nc.semaphore(f"raw_in{s}")) for s in range(4)]
        att = {b: {n: ctx.enter_context(nc.semaphore(f"{n}_{b}")) for n in
                   "tbl stage vt vtok sc ttr exp pd tr pt pv osq st ms rt rc bc out".split()} for b in "ab"}
        X = type("Sems", (), sem)


        def loaded(l, base, i, c):
            return ((l * (CH // 4) + i) + ((base + c) // 4 + 1)) * 16

        block = ctx.enter_context(nc.Block())

        @block.sync
        def _(sp):
            for q in range(4):
                sp.dma_start(h[:, 2 * q:2 * q + 2, :], xT.rearrange("(k p) n -> p k n", p=P)[:, 2 * q:2 * q + 2, :])\
                    .then_inc(x_in[q], 16)
            sp.dma_start(small[:, 104:112], final_g[:, :]).then_inc(X.par_in, 16)

            def chunk(l, base, i, c, src, row, words):
                n = l * CH + (base + c) + i * 4
                sp.wait_ge(X.lo_done, n + 1)
                sp.dma_start(raw[:, c, 0:words], src[bass.ds(row, 1), :, :].rearrange("a p n -> (a p) n"))\
                    .then_inc(raw_in[c], 16)

            def ffn(l, s):
                with sp.Fori(0, KF // 2) as i:
                    for c in range(4):
                        chunk(l, GU[s], i, c, wgu, l * 88 + i * 4 + (44 * s + c), D)
                with sp.Fori(0, KD // 2) as i:
                    for c in range(4):
                        chunk(l, DN[s], i, c, wdn, l * 32 + i * 4 + (16 * s + c), HALF * P)

            with sp.Fori(0, DEPTH) as l:
                ffn(l, 0)
                with sp.Fori(0, 9) as i:
                    for c in range(4):
                        chunk(l, C_P1, i, c, wproj, l * 44 + i * 4 + c, D)
                with sp.Fori(0, 4) as i:
                    chunk(l, C_P3, i, 0, wproj, l * 44 + i * 2 + 36, D)
                    chunk(l, C_P3, i, 1, wmerge, l * 24 + i * 2, SLOT)
                    chunk(l, C_P3, i, 2, wproj, l * 44 + i * 2 + 37, D)
                    chunk(l, C_P3, i, 3, wmerge, l * 24 + i * 2 + 1, SLOT)
                with sp.Fori(0, 4) as i:
                    for c in range(4):
                        chunk(l, C_P4, i, c, wmerge, l * 24 + i * 4 + (8 + c), SLOT)
                with sp.Fori(0, 2) as i:
                    for c in range(4):
                        chunk(l, C_P6, i, c, wout, l * 8 + i * 4 + c, D)
                ffn(l, 1)
            for k in range(KD):
                sp.wait_ge(X.out_ready, k + 1)
                sp.dma_start(out[k * P:(k + 1) * P, :], h_out[:, k, :]).then_inc(X.out_done, 16)
            sp.wait_ge(X.out_done, 16 * KD)

        @block.gpsimd
        def _(pool):
            pool.sem_inc(X.lo_done, 4)

            def split(l, base, i, c, words):
                n = l * CH + (base + c) + i * 4
                pool.wait_ge(raw_in[c], loaded(l, base, i, c))
                pool.wait_ge(X.chunk_done, n + 1)
                pool.nop(nofuse=True)
                w, hi, lo = raw[:, c, 0:words], w_hi[:, c % 2, 0:words], w_lo[:, c % 2, 0:words]
                nc.gpsimd.tensor_scalar(hi, w, 1.0, 0.0, ALU.mult, ALU.add)
                pool.drain()
                nc.gpsimd.tensor_tensor(lo, w, hi.bitcast(F32), ALU.subtract).then_inc(X.lo_done, 1)

            def ffn(l, s):
                with pool.Fori(0, KF // 2) as i:
                    for c in range(4):
                        split(l, GU[s], i, c, D)
                with pool.Fori(0, KD // 2) as i:
                    for c in range(4):
                        split(l, DN[s], i, c, HALF * P)

            with pool.Fori(0, DEPTH) as l:
                ffn(l, 0)
                with pool.Fori(0, 9) as i:
                    for c in range(4):
                        split(l, C_P1, i, c, D)
                with pool.Fori(0, 4) as i:
                    for c in range(4):
                        split(l, C_P3, i, c, SLOT if c % 2 else D)
                with pool.Fori(0, 4) as i:
                    for c in range(4):
                        split(l, C_P4, i, c, SLOT)
                with pool.Fori(0, 2) as i:
                    for c in range(4):
                        split(l, C_P6, i, c, D)
                ffn(l, 1)

        @block.tensor
        def _(pe):
            pe.sem_inc(X.chunk_done, 2)
            for b in "ab":
                pe.sem_inc(att[b]["sc"], 1)
            mm = nc.tensor.matmul

            def block_products(dst, c, blocks, xh, xl, start, stop):
                for b, k in blocks:
                    w1, w2 = w_hi[:, c % 2, b * P:(b + 1) * P], w_lo[:, c % 2, b * P:(b + 1) * P]
                    first, last = start and b == blocks[0][0], stop and b == blocks[-1][0]
                    mm(dst[:, :], w1, xh(k), start=first, stop=False)
                    mm(dst[:, :], w1, xl(k), start=False, stop=False)
                    m = mm(dst[:, :], w2, xh(k), start=False, stop=last)
                return m

            def weights(l, base, i, c, lag):
                n = l * CH + (base + c) + i * 4
                pe.wait_ge(X.lo_done, n + 5)
                if lag:
                    pe.wait_ge(X.prod_taken, n + 5 - lag)

            def phase_start(l, base):
                pe.wait_ge(X.prod_taken, l * CH + base + 4)
                pe.nop(nofuse=True)

            xh, xl = (lambda k: x_hi[:, k, :]), (lambda k: x_lo[:, k, :])

            def product(l, base, i, c, dst, lag=4):
                weights(l, base, i, c, lag)
                block_products(dst, c, [(k, k) for k in range(KD)], xh, xl, True, True)\
                    .then_inc(X.chunk_done, 1)

            def first_product(l, base, i, normed):
                weights(l, base, i, 0, 4)
                for k in range(KD):
                    pe.wait_ge(X.xn_ready, normed + (k + 1))
                    m = block_products(bank[0], 0, [(k, k)], xh, xl, k == 0, k == KD - 1)
                m.then_inc(X.chunk_done, 1)

            def merge(l, base, i, c, gate_bank, branch_bank, yh, yl):
                weights(l, base, i, c, 2)
                block_products(gate_bank, c, [(k, k) for k in range(KD)], xh, xl, True, True)
                block_products(branch_bank, c, [(KD + k, k) for k in range(BRK)],
                               lambda k: yh[:, k, :], lambda k: yl[:, k, :], True, True)\
                    .then_inc(X.chunk_done, 1)

            def token_sums(sq, dst):
                for t in range(TT_):
                    m = mm(dst[:, t:t + 1], sq[:, t * P:(t + 1) * P], ones[:, 0:1], start=True, stop=True)
                return m

            def spread(dst):
                for t in range(TT_):
                    m = mm(dst[:, t * P:(t + 1) * P], rs[:, t:t + 1].broadcast_to([P, P]), ident[:, :],
                           start=True, stop=True)
                return m

            def norm(nu):
                pe.wait_ge(X.sq_added, nu * KD + KD)
                token_sums(sq_sum, bank[7]).then_inc(X.n_stat, 1)
                pe.wait_ge(X.n_rc, nu + 1)
                spread(bank[6]).then_inc(X.n_bc, 1)

            def ffn(l, s):
                phase_start(l, GU[s])
                with pe.Fori(0, KF // 2) as i:
                    for c in range(4):
                        if c == 0:
                            first_product(l, GU[s], i, l * 24 + 16 * s)
                        else:
                            product(l, GU[s], i, c, bank[c])
                with pe.Fori(0, KD // 2) as i:
                    for c in range(4):
                        weights(l, DN[s], i, c, 0 if c % 2 else 4)
                        pe.wait_ge(X.act_ready, l * 44 + (22 * s + (HALF, KF)[c % 2]))
                        block_products(bank[c - c % 2], c, [(k, (c % 2) * HALF + k) for k in range(HALF)],
                                       lambda k: act_hi[:, k, :], lambda k: act_lo[:, k, :],
                                       c % 2 == 0, c % 2 == 1).then_inc(X.chunk_done, 1)

            def transposes(dst, src):
                for b in range(4):
                    m = nc.tensor.transpose(dst[:, b * P:(b + 1) * P], src[:, b * P:(b + 1) * P], ident[:, :])
                return m

            def scores(a, u):
                pe.wait_ge(a["out"], u + 1)
                pe.wait_ge(a["stage"], u + 1)
                transposes(bank[6], v_st).then_inc(a["vt"], 1)
                for g in range(8):
                    m, t = divmod(g, 4)
                    if g >= 2:
                        pe.wait_ge(a["ttr"], u * 8 + (g - 1) + 1)
                    r = slice(64 * m, 64 * m + 64)
                    mm(bank[4 + g % 2][:, :], q_st[r, t * P:(t + 1) * P], k_st[r, :], start=True, stop=True)\
                        .then_inc(a["sc"], 1)

            pe.wait_ge(X.const_in, 32)
            pe.wait_ge(X.pre_lam, 1)
            mm(bank[7][:, 0:4], ones[0:64, :], lamp[0:64, 8:12], start=True, stop=True).then_inc(X.pre_exp, 1)

            with pe.Fori(0, DEPTH) as l:
                norm(l * 3)
                ffn(l, 0)
                norm(l * 3 + 1)
                phase_start(l, C_P1)
                first_product(l, C_P1, 0, l * 24 + 8)
                for c in range(1, 4):
                    product(l, C_P1, 0, c, bank[c])
                sl = lambda t: slice(t * P, (t + 1) * P)

                def level(u, n, lhs, rhs):
                    pe.wait_ge(X.lev_taken, u * 8 + (n + 1))
                    b = bank[4 + n % 2]
                    for t in range(TT_):
                        m = mm(b[:, sl(t)], lhs[:, sl(t)], rhs[:, sl(t)], start=True, stop=True)
                    m.then_inc(X.lev_mm, 1)

                with pe.Fori(0, 4) as i:
                    u = l * 4 + i
                    product(l, C_P2, i * 2, 0, bank[0])
                    pe.wait_ge(X.hg_stage, u + 1)
                    transposes(bank[6], hi_st).then_inc(X.hg_it, 1)
                    pe.wait_ge(X.hg_q64, u + 1)
                    level(u, 0, k_sum, hq)
                    pe.wait_ge(X.lev_taken, u * 8 + 2)
                    for t in range(TT_):
                        a, b = slice(t * P, t * P + CS), slice(t * P + CS, (t + 1) * P)
                        mm(bank[5][0:CS, b], qk64[:, 2, a], qk64[:, 0, b], start=True, stop=True)
                        m = mm(bank[5][CS:P, a], qk64[:, 3, b], qk64[:, 1, a], start=True, stop=True)
                    m.then_inc(X.lev_mm, 1)
                    product(l, C_P2, i * 2, 1, bank[1])
                    pe.wait_ge(X.hg_q128, u + 1)
                    pe.wait_ge(X.hg_itok, u + 1)
                    pe.wait_ge(X.hg_out, u + 1)
                    far = {(0, 2): 0, (1, 3): 1, (0, 3): 2, (3, 1): 3, (2, 0): 4, (3, 0): 5}
                    for a in range(4):
                        if a >= 2:
                            pe.wait_ge(X.od_taken, u * 4 + (a - 1))
                        for b in range(4):
                            if a != b:
                                rhs = q_far[:, far[a, b], :] if (a, b) in far else qk64[:, int(a > b), sl(b)]
                                m = mm(bank[6 + a % 2][:, sl(b)], qk64[:, 2 + int(a > b), sl(a)], rhs,
                                       start=True, stop=True)
                        m.then_inc(X.od_mm, 1)
                        if a == 1:
                            product(l, C_P2, i * 2, 2, bank[2])
                    for j in range(len(LEVELS)):
                        pe.wait_ge(X.lv_mul, u * 6 + (j + 1) + 1)
                        level(u, j + 2, qkl[j % 2][:, 1, :], qkl[j % 2][:, 0, :])
                        if j in (1, 2, 3):
                            product(l, C_P2, i * 2, j + 2, bank[(j + 2) % 4])
                    pe.wait_ge(X.od_taken, u * 4 + 4)
                    pe.wait_ge(X.lev_taken, u * 8 + 10)
                    for a in range(4):
                        m = mm(bank[6][:, :], i_tok[:, sl(a)], AT[:, a, :], start=(a == 0), stop=(a == 3))
                    m.then_inc(X.hg_pv, 1)
                    product(l, C_P2, i * 2, 6, bank[2])
                    pe.wait_ge(X.hg_sq, u + 1)
                    token_sums(ho_sq, bank[7]).then_inc(X.hg_st, 1)
                    product(l, C_P2, i * 2, 7, bank[3])
                    pe.wait_ge(X.hg_rc, u + 1)
                    spread(bank[7]).then_inc(X.hg_bc, 1)
                A = att["a"]
                phase_start(l, C_P3)
                pe.wait_ge(X.hg_out, l * 4 + 4 + 1)
                pe.nop(nofuse=True)
                with pe.Fori(0, 4) as i:
                    u = l * 4 + i
                    scores(A, u)
                    product(l, C_P3, i, 0, bank[0], lag=2)
                    merge(l, C_P3, i, 1, bank[2], bank[3], yc_hi, yc_lo)
                    pe.wait_ge(A["vtok"], u + 1)
                    for t in range(TT_):
                        pe.wait_ge(A["pd"], u * 4 + (t + 1))
                        if t >= 2:
                            pe.wait_ge(A["pt"], u * 4 + (t - 1))
                        transposes(bank[6 + t % 2], S[:, 0, t, :]).then_inc(A["tr"], 1)
                    product(l, C_P3, i, 2, bank[1], lag=2)
                    pe.wait_ge(A["pt"], u * 4 + 4)
                    for k in range(TT_):
                        m = mm(bank[4][:, :], v_tok[:, k * P:(k + 1) * P], pT_a[:, k, :],
                               start=(k == 0), stop=(k == TT_ - 1))
                    m.then_inc(A["pv"], 1)
                    merge(l, C_P3, i, 3, bank[2], bank[3], yc_hi, yc_lo)
                    pe.wait_ge(A["osq"], u + 1)
                    token_sums(o_sq, bank[5]).then_inc(A["st"], 1)
                    pe.wait_ge(A["rc"], u + 1)
                    spread(bank[7]).then_inc(A["bc"], 1)
                B = att["b"]
                phase_start(l, C_P4)
                pe.wait_ge(A["out"], l * 4 + 4 + 1)
                pe.nop(nofuse=True)
                with pe.Fori(0, 2) as i:
                    for r in range(2):
                        u = l * 4 + i * 2 + r
                        scores(B, u)
                        merge(l, C_P4, i, 2 * r, bank[0], bank[1], ya_hi, ya_lo)
                        pe.wait_ge(B["vtok"], u + 1)
                        for g in range(8):
                            pe.wait_ge(B["pd"], u * 8 + (g + 1))
                            if g >= 2:
                                pe.wait_ge(B["pt"], u * 8 + (g - 1))
                            transposes(bank[6 + g % 2], S[:, g // 4, g % 4, :]).then_inc(B["tr"], 1)
                        for m_ in range(2):
                            pe.wait_ge(B["pt"], u * 8 + 4 * (m_ + 1))
                            for k in range(TT_):
                                m = mm(bank[4][64 * m_:64 * m_ + 64, :],
                                       v_tok[:, k * P + 64 * m_:k * P + 64 * m_ + 64], pT_b[m_][:, k, :],
                                       start=(k == 0), stop=(k == TT_ - 1))
                        m.then_inc(B["pv"], 1)
                        merge(l, C_P4, i, 2 * r + 1, bank[2], bank[3], ya_hi, ya_lo)
                phase_start(l, C_P5)
                pe.wait_ge(B["out"], l * 4 + 4 + 1)
                pe.nop(nofuse=True)
                with pe.Fori(0, 2) as i:
                    for c in range(4):
                        merge(l, C_P5, i, c, bank[2 * (c % 2)], bank[2 * (c % 2) + 1], yb_hi, yb_lo)
                phase_start(l, C_P6)
                pe.wait_ge(X.m_ready, l + 1)
                pe.nop(nofuse=True)
                with pe.Fori(0, 2) as i:
                    for c in range(4):
                        weights(l, C_P6, i, c, 4)
                        block_products(bank[c], c, [(k, k) for k in range(KD)], lambda k: m_hi[:, k, :],
                                       lambda k: m_lo[:, k, :], True, True).then_inc(X.chunk_done, 1)
                norm(l * 3 + 2)
                ffn(l, 1)
            norm(DEPTH * 3)

        @block.scalar
        def _(act):
            A_ = nc.scalar.activation
            act.dma_start(ident[:, :], ident_c[:, :]).then_inc(X.const_in, 16)
            act.dma_start(mask_f[:, :, :], masks_c.rearrange("p (j n) -> p j n", n=P)).then_inc(X.const_in, 16)
            act.dma_start(par2[:, :].rearrange("p (l c) -> p l c", l=DEPTH)[:, :, 0:26], gains[:, :, :])\
                .then_inc(X.par_in, 16)
            act.dma_start(lbr, lb_raw[:, :]).then_inc(X.par_in, 16)
            act.dma_start(lamp[0:64, 0:8], lam_in[:, :]).then_inc(X.par_in, 16)
            act.wait_ge(X.pre_exp, 1)
            act.wait_ge(X.pre_lam, 2)
            A_(lamp[:, 12:16], bank[7][:, 0:4], ACT.Exp)
            A_(lbt[:, 0:8], lbr, ACT.Exp)
            act.drain().then_inc(X.pre_exp, 1)

            def norm(nu):
                for k in range(KD):
                    act.wait_ge(X.h_upd, nu * KD + (k + 1))
                    if k >= 2:
                        act.wait_ge(X.sq_added, nu * KD + (k - 1))
                    A_(h_sq[:, k % 2, :], h[:, k, :], ACT.Square).then_inc(X.sq_ready, 1)
                A_(warm, ones[:, 0:1], ACT.Sqrt)
                act.wait_ge(X.n_ms, nu + 1)
                A_(rt, ms, ACT.Sqrt).then_inc(X.n_rt, 1)

            def halves(nx):
                for k in range(KD):
                    act.wait_ge(X.xf_ready, nx * KD + (k + 1))
                    A_(x_hi[:, k, :], x_f[:, k % 2, :], ACT.Copy).then_inc(X.xhi_ready, 1)

            def ffn(l, s):
                with act.Fori(0, KF // 2) as i:
                    for v in range(2):
                        n = l * CH + (GU[s] + 2 * v) + i * 4
                        act.wait_ge(X.chunk_done, n + 3)
                        act.wait_ge(X.prod_taken, n + 2)
                        A_(silu_g[:, v, :], bank[2 * v][:, :], ACT.Silu).then_inc(X.silu_done, 1)

            def take(l, base, i, c, slot):
                n = l * CH + (base + c) + i * 4
                act.wait_ge(X.chunk_done, n + 3)
                act.nop(nofuse=True)
                A_(z[:, bass.ds(slot, 1), :].rearrange("p a n -> p (a n)"), bank[c % 4][:, :], ACT.Copy)\
                    .then_inc(X.prod_taken, 1)

            def gate(l, base, i, c, b, count):
                n = l * CH + (base + c) + i * 4
                act.wait_ge(X.chunk_done, n + 3)
                act.wait_ge(X.gate_done, count + 1)
                A_(gate_t[:, :], bank[b][:, :], ACT.Tanh, scale=0.5).then_inc(X.gate_ready, 1)

            def stage(dst, slot):
                return A_(dst[:, :], z[:, bass.ds(slot, 1), :].rearrange("p a n -> p (a n)"), ACT.Copy)

            def attention_in(a, u, tables, qkv):
                act.wait_ge(a["ttr"], u * 8 + 1)
                for m, row in enumerate(tables):
                    act.dma_start(bias[:, m, :], bias_c[bass.ds(row, 1), :, :].rearrange("a p n -> (a p) n"))\
                        .then_inc(a["tbl"], 16)
                act.wait_ge(a["sc"], u * 8 + 1)
                act.nop(nofuse=True)
                for dst, slot in zip((q_st, k_st, v_st), qkv):
                    stage(dst, slot)
                act.drain().then_inc(a["stage"], 1)
                act.wait_ge(a["vt"], u + 1)
                A_(v_tok[:, :], bank[6][:, :], ACT.Copy).then_inc(a["vtok"], 1)
                for g in range(8):
                    act.wait_ge(a["ttr"], u * 8 + (g + 1) + 1)
                    A_(S[:, g // 4, g % 4, :], S[:, g // 4, g % 4, :], ACT.Exp, bias=neg_max[:, g:g + 1],
                       scale=-1.0, accum_out=p_sum[:, g:g + 1]).then_inc(a["exp"], 1)

            def p_columns(a, u, n, g, dst):
                t = g % 4
                act.wait_ge(a["tr"], u * n + (g + 1))
                A_(dst[:, :, t * P:(t + 1) * P], bank[6 + g % 2][:, :].rearrange("p (k n) -> p k n", n=P),
                   ACT.Copy).then_inc(a["pt"], 1)

            with act.Fori(0, DEPTH) as l:
                norm(l * 3)
                halves(l * 3)
                ffn(l, 0)
                norm(l * 3 + 1)
                halves(l * 3 + 1)
                act.wait_ge(X.xn_ready, l * 24 + 16)
                act.dma_start(h_save.rearrange("(k p) n -> p k n", p=P), h[:, :, :]).then_inc(X.h_saved, 16)
                for c in range(4):
                    take(l, C_P1, 0, c, 5 * c)

                def lv(u, j):
                    act.wait_ge(X.lv_sub, u * 6 + (j + 1))
                    A_(xy[j % 2][:, :, :], xy[j % 2][:, :, :], ACT.Exp).then_inc(X.lv_exp, 1)

                def head_start(i, u, taken):
                    act.wait_ge(X.prod_taken, taken)
                    act.wait_ge(X.lv_mul, u * 6 + 1)
                    act.nop(nofuse=True)
                    stage(hq, i + 10)
                    stage(hi_st, i + 15)
                    act.drain().then_inc(X.hg_stage, 1)
                    act.wait_ge(X.hg_nf, u + 1)
                    A_(kk[:, :, :], nf[:, :, :], ACT.Exp)
                    act.drain()
                    A_(ln1[:, :, :], kk[:, :, :], ACT.Ln, bias=1.0)
                    A_(gg[:, :, :], kk[:, :, :], ACT.Ln, bias=1.0, scale=lb_h[:, 0:1])
                    act.drain().then_inc(X.hg_ln, 1)
                    act.wait_ge(X.hg_ar, u + 1)
                    A_(kk[:, :, :], nf[:, :, :], ACT.Exp).then_inc(X.hg_kexp, 1)

                def head_exps(u):
                    act.wait_ge(X.hg_rem, u + 1)
                    A_(qk64[:, 0:2, :], run[:, :, :], ACT.Exp)
                    A_(qk64[:, 2:4, :], qk64[:, 2:4, :], ACT.Exp)
                    act.drain().then_inc(X.hg_e, 1)
                    lv(u, 0)
                    lv(u, 1)

                def head(i, last):
                    u = l * 4 + i
                    act.wait_ge(X.hg_it, u + 1)
                    A_(i_tok[:, :], bank[6][:, :], ACT.Copy).then_inc(X.hg_itok, 1)
                    take(l, C_P2, i * 2, 0, i + 20)
                    take(l, C_P2, i * 2, 1, i + 1)
                    for a in range(4):
                        if a == 2:
                            take(l, C_P2, i * 2, 2, i + 6)
                        act.wait_ge(X.od_mm, u * 4 + (a + 1))
                        for lo_, hi_ in ((0, a), (a + 1, 4)):
                            if hi_ > lo_:
                                A_(AT[:, a, lo_ * P:hi_ * P], bank[6 + a % 2][:, lo_ * P:hi_ * P], ACT.Copy)
                        act.drain().then_inc(X.od_taken, 1)
                    lv(u, 2)
                    lv(u, 3)
                    take(l, C_P2, i * 2, 3, i + 11)
                    lv(u, 4)
                    take(l, C_P2, i * 2, 4, i + 16)
                    lv(u, 5)
                    act.wait_ge(X.hg_out, u + 1)
                    act.nop(nofuse=True)
                    A_(og_t[:, :], z[:, bass.ds(i + 20, 1), :].rearrange("p a n -> p (a n)"), ACT.Tanh, scale=0.5)\
                        .then_inc(X.hg_og, 1)
                    take(l, C_P2, i * 2, 5, i + 24)
                    if not last:
                        head_start(i + 1, u + 1, l * CH + (C_P2 + 5 + 4) + i * 8)
                    act.wait_ge(X.hg_pv, u + 1)
                    A_(ho_sq[:, :], bank[6][:, :], ACT.Square)
                    A_(ho_f[:, :], bank[6][:, :], ACT.Copy)
                    act.drain().then_inc(X.hg_sq, 1)
                    if not last:
                        head_exps(u + 1)
                    take(l, C_P2, i * 2, 6, i + 28)
                    act.wait_ge(X.hg_ms, u + 1)
                    A_(rt, ms, ACT.Sqrt).then_inc(X.hg_rt, 1)
                    take(l, C_P2, i * 2, 7, i + 32)

                head_start(0, l * 4, l * CH + (C_P1 + 4 + 4))
                head_exps(l * 4)
                with act.Fori(0, 3) as i:
                    head(i, False)
                head(3, True)
                A = att["a"]
                act.wait_ge(X.hg_out, l * 4 + 4 + 1)
                act.wait_ge(X.prod_taken, l * CH + (C_P3 + 4))
                act.nop(nofuse=True)
                with act.Fori(0, 4) as i:
                    u = l * 4 + i
                    attention_in(A, u, [i], (i + 24, i + 28, i + 32))
                    gate(l, C_P3, i, 1, 2, l * 24 + i * 2)
                    act.wait_ge(A["pd"], u * 4 + 4)
                    for t in range(TT_):
                        p_columns(A, u, 4, t, pT_a)
                    act.wait_ge(A["pv"], u + 1)
                    A_(o_sq[:, :], bank[4][:, :], ACT.Square)
                    A_(o_f[:, :], bank[4][:, :], ACT.Copy)
                    act.drain().then_inc(A["osq"], 1)
                    gate(l, C_P3, i, 3, 2, l * 24 + i * 2 + 1)
                    act.wait_ge(A["ms"], u + 1)
                    A_(rt, ms, ACT.Sqrt).then_inc(A["rt"], 1)
                B = att["b"]
                act.wait_ge(A["out"], l * 4 + 4 + 1)
                act.wait_ge(X.prod_taken, l * CH + (C_P4 + 4))
                act.nop(nofuse=True)
                with act.Fori(0, 2) as i:
                    for r in range(2):
                        u = l * 4 + i * 2 + r
                        p = i * 2 + r
                        attention_in(B, u, [i * 4 + (4 + 2 * r), i * 4 + (5 + 2 * r)],
                                     (p * 5 + 4, p + 36, p + 40))
                        gate(l, C_P4, i, 2 * r, 0, l * 24 + i * 4 + (8 + 2 * r))
                        for g in range(8):
                            p_columns(B, u, 8, g, pT_b[g // 4])
                        gate(l, C_P4, i, 2 * r + 1, 2, l * 24 + i * 4 + (9 + 2 * r))
                act.wait_ge(B["out"], l * 4 + 4 + 1)
                act.wait_ge(X.h_saved, l * 16 + 16)
                act.dma_start(h[:, :, :], h_save.rearrange("(k p) n -> p k n", p=P)).then_inc(X.h_back, 16)
                with act.Fori(0, 2) as i:
                    for c in range(4):
                        gate(l, C_P5, i, c, 2 * (c % 2), l * 24 + i * 4 + (16 + c))
                norm(l * 3 + 2)
                halves(l * 3 + 2)
                ffn(l, 1)
            norm(DEPTH * 3)

        @block.vector
        def _(dve):
            V = nc.vector
            dve.sem_inc(X.prod_taken, 4)
            dve.sem_inc(X.lev_taken, 2)
            for s in (X.hg_out, X.lv_mul, X.gate_done, att["a"]["ttr"], att["a"]["out"], att["b"]["ttr"], att["b"]["out"]):
                dve.sem_inc(s, 1)
            V.memset(ones[:, :], 1.0)
            V.memset(run_mask[:, :], 1.0)
            dve.wait_ge(X.par_in, 64)
            V.tensor_tensor(lamp[0:64, 8:10], lamp[0:64, 0:2], lamp[0:64, 2:4], ALU.mult)
            V.tensor_tensor(lamp[0:64, 10:12], lamp[0:64, 4:6], lamp[0:64, 6:8], ALU.mult)
            dve.drain().then_inc(X.pre_lam, 1)
            V.memset(run_mask[:, :].rearrange("p (c t) -> p c t", t=CS)[:, :, 0:1], 0.0)
            V.tensor_tensor(lbt[:, 8:12], lbr[:, 0:4], lbr[:, 4:8], ALU.max)
            dve.drain()
            V.tensor_tensor(lbr[:, 0:4], lbr[:, 0:4], lbt[:, 8:12], ALU.subtract)
            V.tensor_tensor(lbr[:, 4:8], lbr[:, 4:8], lbt[:, 8:12], ALU.subtract)
            dve.drain().then_inc(X.pre_lam, 1)
            dve.wait_ge(X.pre_exp, 2)
            V.tensor_tensor(lbt[:, 8:12], lbt[:, 0:4], lbt[:, 4:8], ALU.add)
            V.tensor_tensor(lamp[:, 16:18], lamp[:, 14:16], lamp[:, 12:14], ALU.subtract)
            dve.drain()
            V.reciprocal(lbt[:, 8:12], lbt[:, 8:12])
            dve.drain()
            for l in range(DEPTH):
                p0 = l * NPAR
                lam_init = 0.8 - 0.6 * float(np.exp(-0.3 * l))
                if l == 0:
                    V.memset(par2[:, p0 + LB:p0 + LB + 4], 0.0)
                else:
                    V.tensor_tensor(par2[:, p0 + LB:p0 + LB + 4], lbt[:, 4:8], lbt[:, 8:12], ALU.mult)
                V.tensor_scalar(par2[:, p0 + NLAM:p0 + NLAM + 1], lamp[:, 16 + l:17 + l], -lam_init, None, ALU.add)
                V.tensor_scalar(par2[:, p0 + G_SUB:p0 + G_SUB + 1], par2[:, p0 + G_SUB:p0 + G_SUB + 1],
                                1.0 - lam_init, None, ALU.mult)
                V.tensor_scalar(par2[:, p0 + G_HG:p0 + G_HG + 1], par2[:, p0 + G_HG:p0 + G_HG + 1],
                                0.5, None, ALU.mult)
            dve.drain()
            for l in range(DEPTH):
                p0 = l * NPAR
                V.tensor_scalar(par2[:, p0 + OMLB:p0 + OMLB + 4], par2[:, p0 + LB:p0 + LB + 4],
                                -1.0, 1.0, ALU.mult, ALU.add)
            V.memset(par2[:, NLAM + 1:NLAM + 2], 0.0)
            V.memset(par2[:, NPAR + NLAM + 1:NPAR + NLAM + 2], 0.0)
            dve.drain()
            V.memset(sq_sum[:, :], 0.0)
            dve.drain()

            def add_square(v, tile):
                dve.wait_ge(X.sq_ready, tile + 1)
                V.tensor_tensor(sq_sum[:, :], h_sq[:, v, :], sq_sum[:, :], ALU.add)
                dve.drain().then_inc(X.sq_added, 1)

            for k in range(KD):
                if k % 2 == 0:
                    dve.wait_ge(x_in[k // 2], 16)
                    dve.sem_inc(X.h_upd, 2)
                add_square(k % 2, k)
            dve.wait_ge(X.const_in, 32)
            V.tensor_copy(masks[:, :, :].rearrange("p j (a n) -> p j a n", n=P),
                          mask_f[:, :, :].rearrange("p j (a n) -> p j a n", a=1)
                          .broadcast_to([P, len(LEVELS), TT_, P]))
            dve.drain()

            def inverse_rms(width, stat, done_ms, rt_in, done_rc, nu, ready):
                dve.wait_ge(ready, nu + 1)
                V.tensor_scalar(ms, stat[:, 0:4], 1.0 / width, EPS, ALU.mult, ALU.add).then_inc(done_ms, 1)
                dve.wait_ge(rt_in, nu + 1)
                V.reciprocal(rs, rt).then_inc(done_rc, 1)

            def norm(nu, g0):
                inverse_rms(D, bank[7], X.n_ms, X.n_rt, X.n_rc, nu, X.n_stat)
                dve.wait_ge(X.n_bc, nu + 1)
                for k in range(KD + 1):
                    if k < KD:
                        V.scalar_tensor_tensor(x_f[:, k % 2, :], h[:, k, :], par[:, g0 + k:g0 + k + 1],
                                               bank[6][:, :], ALU.mult, ALU.mult).then_inc(X.xf_ready, 1)
                    if k >= 1:
                        dve.wait_ge(X.xhi_ready, nu * KD + k)
                        V.tensor_tensor(x_lo[:, k - 1, :], x_f[:, (k - 1) % 2, :],
                                        x_hi[:, k - 1, :].bitcast(F32), ALU.subtract)
                        dve.drain().then_inc(X.xn_ready, 1)

            def ffn(l, s):
                with dve.Fori(0, KF // 2) as i:
                    for v in range(2):
                        n = l * CH + (GU[s] + 2 * v + 1) + i * 4
                        f = i * 2 + v
                        dve.wait_ge(X.chunk_done, n + 3)
                        dve.wait_ge(X.silu_done, l * 44 + i * 2 + (22 * s + v + 1))
                        V.tensor_tensor(act_f[:, v, :], silu_g[:, v, :], bank[2 * v + 1][:, :], ALU.mult)
                        dve.drain().then_inc(X.prod_taken, 2)
                        hi = act_hi[:, bass.ds(f, 1), :].rearrange("p a n -> p (a n)")
                        lo = act_lo[:, bass.ds(f, 1), :].rearrange("p a n -> p (a n)")
                        V.tensor_copy(hi, act_f[:, v, :])
                        dve.drain()
                        V.tensor_tensor(lo, act_f[:, v, :], hi.bitcast(F32), ALU.subtract)
                        dve.drain().then_inc(X.act_ready, 1)
                V.memset(sq_sum[:, :], 0.0)
                dve.drain()
                with dve.Fori(0, KD // 2) as i:
                    for v in range(2):
                        n = l * CH + (DN[s] + 2 * v + 1) + i * 4
                        dve.wait_ge(X.chunk_done, n + 3)
                        hj = h[:, bass.ds(i * 2 + v, 1), :].rearrange("p a n -> p (a n)")
                        V.scalar_tensor_tensor(hj, bank[2 * v][:, :], 0.5, hj, ALU.mult, ALU.add)\
                            .then_inc(X.h_upd, 1)
                        dve.drain().then_inc(X.prod_taken, 2)
                        add_square(v, l * 24 + i * 2 + (8 + 16 * s + v))

            def take(l, base, i, c, b, slot):
                n = l * CH + (base + c) + i * 4
                dve.wait_ge(X.chunk_done, n + 3)
                dve.nop(nofuse=True)
                V.tensor_copy(z[:, bass.ds(slot, 1), :].rearrange("p a n -> p (a n)"), bank[b][:, :])\
                    .then_inc(X.prod_taken, 1)

            def gated_sum(l, base, i, c, b, count, j, how):
                dve.wait_ge(X.gate_ready, count + 1)
                dve.wait_ge(X.chunk_done, l * CH + (base + c + 3) + i * 4)
                mj = merged[:, bass.ds(j, 1), :].rearrange("p a n -> p (a n)")
                dst = mj if how == "first" else gated[:, :]
                V.scalar_tensor_tensor(dst, gate_t[:, :], 1.0, bank[b][:, :], ALU.add, ALU.mult)
                dve.drain().then_inc(X.prod_taken, 1)
                if how == "first":
                    dve.sem_inc(X.gate_done, 1)
                    return
                V.tensor_tensor(mj if how == "more" else gated[:, :], gated[:, :], mj, ALU.add)
                dve.drain().then_inc(X.gate_done, 1)
                if how == "last":
                    mh = m_hi[:, bass.ds(j, 1), :].rearrange("p a n -> p (a n)")
                    ml = m_lo[:, bass.ds(j, 1), :].rearrange("p a n -> p (a n)")
                    V.tensor_scalar(mh, gated[:, :], 0.5, None, ALU.mult)
                    dve.drain()
                    V.scalar_tensor_tensor(ml, gated[:, :], 0.5, mh.bitcast(F32), ALU.mult, ALU.subtract)
                    dve.drain()

            def row_max(a, u, tables):
                dve.wait_ge(a["tbl"], (u + 1) * (16 * tables))
                for g in range(8):
                    m, t = divmod(g, 4)
                    dve.wait_ge(a["sc"], u * 8 + (g + 1) + 1)
                    dve.nop(nofuse=True)
                    V.tensor_tensor_reduce(out=S[:, m, t, :], in0=bank[4 + g % 2][:, :],
                                           in1=bias[:, m if tables == 2 else 0, 384 - t * P:384 - t * P + SEQ],
                                           scale=-SCALE, scalar=3.0e38, op0=ALU.add, op1=ALU.min,
                                           accum_out=neg_max[:, g:g + 1])
                    dve.drain().then_inc(a["ttr"], 1)
                dve.wait_ge(a["exp"], u * 8 + 8)
                V.reciprocal(p_rs, p_sum)
                dve.drain()

            def split(hi, lo, src):
                V.tensor_copy(hi, src)
                dve.drain()
                V.tensor_tensor(lo, src, hi.bitcast(F32), ALU.subtract)

            tile_of = lambda t, j: t[:, bass.ds(j, 1), :].rearrange("p a n -> p (a n)")

            with dve.Fori(0, DEPTH) as l:
                V.tensor_copy(par, par2[:, bass.ds(l * NPAR, NPAR)])
                dve.drain()
                norm(l * 3, G_FFN1)
                ffn(l, 0)
                norm(l * 3 + 1, G_MIX)
                dve.wait_ge(X.h_saved, l * 16 + 16)
                dve.nop(nofuse=True)
                rc = lambda t: t.rearrange("p (c t) -> p c t", t=CS)
                sl = lambda t: slice(t * P, (t + 1) * P)

                def halves_of(t, m):
                    return t.rearrange("p (b s m) -> p b s m", s=2, m=m)

                def level_sub(j):
                    m = LEVELS[j]
                    nb = SEQ // (2 * m)
                    x, y = halves_of(xy[j % 2][:, 0, :], m), halves_of(xy[j % 2][:, 1, :], m)
                    rf, rb = halves_of(run[:, 0, :], m), halves_of(run[:, 1, :], m)
                    cf = rf[:, :, 0, m - 1:m].broadcast_to([P, nb, m])
                    cb = rb[:, :, 1, 0:1].broadcast_to([P, nb, m])
                    V.tensor_tensor(x[:, :, 1, :], rf[:, :, 1, :], cf, ALU.subtract)
                    V.tensor_tensor(y[:, :, 0, :], cf, rf[:, :, 0, :], ALU.subtract)
                    V.tensor_tensor(x[:, :, 0, :], rb[:, :, 0, :], cb, ALU.subtract)
                    V.tensor_tensor(y[:, :, 1, :], cb, rb[:, :, 1, :], ALU.subtract)
                    dve.drain().then_inc(X.lv_sub, 1)

                def level_mul(u, j):
                    m = LEVELS[j]
                    dve.wait_ge(X.lv_exp, u * 6 + (j + 1))
                    dve.wait_ge(X.lev_mm, u * 8 + (j + 1))
                    e, o = xy[j % 2], qkl[j % 2]
                    V.tensor_tensor(o[:, 0, :], e[:, 0, :], hq[:, :], ALU.mult)
                    for s in range(2):
                        V.tensor_tensor(halves_of(o[:, 1, :], m)[:, :, s, :], halves_of(e[:, 1, :], m)[:, :, s, :],
                                        halves_of(kk[:, s, :], m)[:, :, s, :], ALU.mult)
                    dve.drain().then_inc(X.lv_mul, 1)

                def level_take(u, j):
                    dve.wait_ge(X.lev_mm, u * 8 + (j + 3))
                    dve.nop(nofuse=True)
                    V.copy_predicated(ATd, masks[:, j, :].rearrange("p (a n) -> p a n", n=P),
                                      bank[4 + j % 2][:, :].rearrange("p (a n) -> p a n", n=P))
                    dve.drain().then_inc(X.lev_taken, 1)

                def head_gates(i, u, taken):
                    dve.wait_ge(X.prod_taken, taken)
                    dve.nop(nofuse=True)
                    f2 = z[:, 0:10, :].rearrange("p (d a) n -> p d a n", d=2)[:, :, bass.ds(i, 1), :]\
                        .rearrange("p d a n -> p d (a n)")
                    V.tensor_copy(lb_h[:, 0:1], par[:, bass.ds(i + LB, 1)])
                    V.tensor_copy(lb_h[:, 1:2], par[:, bass.ds(i + OMLB, 1)])
                    V.tensor_scalar(nf[:, :, :], f2, -1.0, F_CAP, ALU.mult, ALU.min)
                    dve.drain().then_inc(X.hg_nf, 1)
                    dve.wait_ge(X.hg_ln, u + 1)
                    V.tensor_tensor(nf[:, :, :], nf[:, :, :], ln1[:, :, :], ALU.subtract)
                    V.tensor_tensor(gg[:, :, :], gg[:, :, :], ln1[:, :, :], ALU.subtract)
                    dve.drain().then_inc(X.hg_ar, 1)
                    V.tensor_tensor_scan(run[:, 0, :], run_mask[:, :], gg[:, 0, :], 0.0, ALU.mult, ALU.add)
                    V.tensor_tensor_scan(run[:, 1, ::-1], run_mask[:, :], gg[:, 1, ::-1], 0.0, ALU.mult, ALU.add)
                    dve.drain()
                    V.tensor_tensor(rc(qk64[:, 2, :]), rc(run[:, 0, :])[:, :, CS - 1:CS].broadcast_to([P, NC, CS]),
                                    rc(run[:, 0, :]), ALU.subtract)
                    V.tensor_tensor(rc(qk64[:, 3, :]), rc(run[:, 1, :])[:, :, 0:1].broadcast_to([P, NC, CS]),
                                    rc(run[:, 1, :]), ALU.subtract)
                    dve.drain().then_inc(X.hg_rem, 1)
                    dve.wait_ge(X.hg_kexp, u + 1)
                    V.tensor_scalar(kk[:, :, :], kk[:, :, :], lb_h[:, 1:2], None, ALU.mult)
                    dve.drain()
                    V.tensor_tensor(k_sum[:, :], kk[:, 0, :], kk[:, 1, :], ALU.add)
                    level_sub(0)
                    level_sub(1)

                def head_decays(u):
                    dve.wait_ge(X.hg_stage, u + 1)
                    dve.wait_ge(X.hg_e, u + 1)
                    V.tensor_copy(tot[:, 0:8], rc(qk64[:, 0, :])[:, :, CS - 1])
                    V.tensor_copy(tot[:, 8:16], rc(qk64[:, 1, :])[:, :, 0])
                    dve.drain()
                    V.tensor_tensor(qk64[:, 0:2, :], qk64[:, 0:2, :],
                                    hq[:, :].rearrange("p (a n) -> p a n", a=1).broadcast_to([P, 2, SEQ]), ALU.mult)
                    V.tensor_tensor(qk64[:, 2:4, :], qk64[:, 2:4, :], kk[:, :, :], ALU.mult)
                    tv = tot.rearrange("p (a s) -> p a s", s=2)
                    V.tensor_tensor(ttot, tv[:, :, 0], tv[:, :, 1], ALU.mult)
                    dve.drain().then_inc(X.hg_q64, 1)

                def head(i, last):
                    u = l * 4 + i
                    dve.wait_ge(X.lev_mm, u * 8 + 1)
                    V.tensor_copy(ATd, bank[4][:, :].rearrange("p (a n) -> p a n", n=P))
                    dve.drain().then_inc(X.lev_taken, 1)
                    dve.wait_ge(X.lev_mm, u * 8 + 2)
                    b5 = bank[5][:, :].rearrange("p (a n) -> p a n", n=P)
                    V.tensor_copy(ATd[0:CS, :, CS:P], b5[0:CS, :, CS:P])
                    V.tensor_copy(ATd[CS:P, :, 0:CS], b5[CS:P, :, 0:CS])
                    dve.drain().then_inc(X.lev_taken, 1)
                    r4 = lambda t: t.rearrange("p (a s n) -> p a s n", s=2, n=CS)
                    for row, outer, d in ((0, 1, 0), (2, 0, 0), (1, 0, 1), (3, 1, 1)):
                        t_in = tot[:, 8 * d:8 * d + 8].rearrange("p (a s) -> p a s", s=2)[:, :, 1 - outer:2 - outer]
                        v = r4(qk64[:, row, :])[:, :, outer, :]
                        V.tensor_tensor(v, v, t_in.broadcast_to([P, TT_, CS]), ALU.mult)
                    dve.drain()
                    sc = lambda d, t: ttot[:, 4 * d + t:4 * d + t + 1]
                    V.tensor_scalar(q_far[:, 0, :], qk64[:, 0, sl(2)], sc(0, 1), None, ALU.mult)
                    V.tensor_scalar(q_far[:, 1, :], qk64[:, 0, sl(3)], sc(0, 2), None, ALU.mult)
                    V.tensor_scalar(q_far[:, 3, :], qk64[:, 1, sl(1)], sc(1, 2), None, ALU.mult)
                    V.tensor_scalar(q_far[:, 4, :], qk64[:, 1, sl(0)], sc(1, 1), None, ALU.mult)
                    dve.drain()
                    V.tensor_scalar(q_far[:, 2, :], q_far[:, 1, :], sc(0, 1), None, ALU.mult)
                    V.tensor_scalar(q_far[:, 5, :], q_far[:, 4, :], sc(1, 2), None, ALU.mult)
                    dve.drain().then_inc(X.hg_q128, 1)
                    for j in range(len(LEVELS)):
                        level_mul(u, j)
                        if j + 2 < len(LEVELS):
                            level_sub(j + 2)
                        if j >= 1:
                            level_take(u, j - 1)
                    level_take(u, len(LEVELS) - 1)
                    if not last:
                        head_gates(i + 1, u + 1, l * CH + (C_P2 + 3 + 4) + i * 8)
                    dve.wait_ge(X.hg_og, u + 1)
                    V.scalar_tensor_tensor(og_t[:, :], og_t[:, :], 1.0, tile_of(z, i + 20), ALU.add, ALU.mult)
                    inverse_rms(P, bank[7], X.hg_ms, X.hg_rt, X.hg_rc, u, X.hg_st)
                    if not last:
                        head_decays(u + 1)
                    dve.wait_ge(X.hg_bc, u + 1)
                    V.scalar_tensor_tensor(ho_f[:, :], ho_f[:, :], par[:, G_HG:G_HG + 1], bank[7][:, :],
                                           ALU.mult, ALU.mult)
                    dve.drain()
                    V.tensor_tensor(ho_f[:, :], ho_f[:, :], og_t[:, :], ALU.mult)
                    dve.drain()
                    split(tile_of(yc_hi, i), tile_of(yc_lo, i), ho_f[:, :])
                    dve.drain().then_inc(X.hg_out, 1)

                head_gates(0, l * 4, l * CH + (C_P1 + 2 + 4))
                head_decays(l * 4)
                with dve.Fori(0, 3) as i:
                    head(i, False)
                head(3, True)
                A = att["a"]
                with dve.Fori(0, 4) as i:
                    u = l * 4 + i
                    row_max(A, u, 1)
                    V.tensor_scalar(p_c2, p_rs[:, 4:8], par[:, NLAM:NLAM + 1], None, ALU.mult)
                    for t in range(TT_):
                        V.tensor_scalar(S[:, 0, t, :], S[:, 0, t, :], p_rs[:, t:t + 1], None, ALU.mult)
                    dve.drain()
                    for t in range(TT_):
                        V.scalar_tensor_tensor(S[:, 0, t, :], S[:, 1, t, :], p_c2[:, t:t + 1], S[:, 0, t, :],
                                               ALU.mult, ALU.add).then_inc(A["pd"], 1)
                    take(l, C_P3, i, 0, 0, i + 36)
                    gated_sum(l, C_P3, i, 1, 3, l * 24 + i * 2, i * 2, "first")
                    take(l, C_P3, i, 2, 1, i + 40)
                    gated_sum(l, C_P3, i, 3, 3, l * 24 + i * 2 + 1, i * 2 + 1, "first")
                    inverse_rms(P, bank[5], A["ms"], A["rt"], A["rc"], u, A["st"])
                    dve.wait_ge(A["bc"], u + 1)
                    V.scalar_tensor_tensor(o_f[:, :], o_f[:, :], par[:, G_SUB:G_SUB + 1], bank[7][:, :],
                                           ALU.mult, ALU.mult)
                    dve.drain()
                    split(tile_of(ya_hi, i), tile_of(ya_lo, i), o_f[:, :])
                    dve.drain().then_inc(A["out"], 1)
                B = att["b"]
                with dve.Fori(0, 2) as i:
                    for r in range(2):
                        u = l * 4 + i * 2 + r
                        row_max(B, u, 2)
                        for g in range(8):
                            V.tensor_scalar(S[:, g // 4, g % 4, :], S[:, g // 4, g % 4, :], p_rs[:, g:g + 1],
                                            None, ALU.mult).then_inc(B["pd"], 1)
                        gated_sum(l, C_P4, i, 2 * r, 1, l * 24 + i * 4 + (8 + 2 * r), i * 4 + 2 * r, "more")
                        dve.wait_ge(B["pv"], u + 1)
                        split(tile_of(yb_hi, i * 2 + r), tile_of(yb_lo, i * 2 + r), bank[4][:, :])
                        dve.drain().then_inc(B["out"], 1)
                        gated_sum(l, C_P4, i, 2 * r + 1, 3, l * 24 + i * 4 + (9 + 2 * r), i * 4 + 2 * r + 1, "more")
                with dve.Fori(0, 2) as i:
                    for c in range(4):
                        gated_sum(l, C_P5, i, c, 2 * (c % 2) + 1, l * 24 + i * 4 + (16 + c), i * 4 + c, "last")
                dve.drain().then_inc(X.m_ready, 1)
                V.memset(sq_sum[:, :], 0.0)
                dve.drain()
                dve.wait_ge(X.h_back, l * 16 + 16)
                dve.nop(nofuse=True)
                with dve.Fori(0, 2) as i:
                    for c in range(4):
                        dve.wait_ge(X.chunk_done, l * CH + (C_P6 + c + 3) + i * 4)
                        hj = tile_of(h, i * 4 + c)
                        V.tensor_tensor(hj, bank[c][:, :], hj, ALU.add).then_inc(X.h_upd, 1)
                        dve.drain().then_inc(X.prod_taken, 1)
                        add_square(c % 2, l * 24 + i * 4 + (16 + c))
                norm(l * 3 + 2, G_FFN2)
                ffn(l, 1)
            nu = DEPTH * 3
            inverse_rms(D, bank[7], X.n_ms, X.n_rt, X.n_rc, nu, X.n_stat)
            dve.wait_ge(X.n_bc, nu + 1)
            for k in range(KD):
                V.scalar_tensor_tensor(h_out[:, k, :], h[:, k, :], fin_g[:, k:k + 1], bank[6][:, :],
                                       ALU.mult, ALU.mult).then_inc(X.out_ready, 1)


def alibi_tables():
    n = 12
    slopes = np.exp2(np.float32(-8.0) * np.arange(1, n + 1, dtype=np.float32) / np.float32(n)).astype(np.float32)
    d = np.arange(UW)[None, :] - 384 - np.arange(P)[:, None]
    dist = np.abs(d)
    count = np.zeros(d.shape, np.int64)
    for window, dilation in ((128, 1), (512, 4), (2048, 16)):
        count += (dist % dilation == 0) & (dist // dilation <= window // (2 * dilation))
    ln_count = np.where(count > 0, np.log(np.maximum(count, 1)), -1e30)
    out = np.zeros((n, P, UW), np.float32)
    for row, s in enumerate((0, 3, 6, 9, 1, 2, 4, 5, 7, 8, 10, 11)):
        b = (-slopes[s] * dist.astype(np.float32)).astype(np.float64)
        out[row] = ((b + (ln_count if row >= 4 else 0)) / SCALE).astype(np.float32)
    return out


def level_masks():
    s, t = np.arange(P)[:, None], np.arange(P)[None, :]
    rows = [((s // (2 * m) == t // (2 * m)) & (s // m != t // m)) for m in LEVELS]
    return np.concatenate(rows, axis=1).astype(np.float32)


def kernel(**inputs):
    import concourse.bacc as bacc
    from concourse.bass_utils import run_bass_kernel_spmd

    a = {k: np.asarray(v) for k, v in inputs.items()}

    def blocks(w, cols):
        k, n = w.shape
        b = w.reshape(k // P, P, n // P, P).transpose(2, 1, 0, 3)
        return b[cols]

    def chunks(w, cols):
        b = blocks(w, cols)
        return b.reshape(b.shape[0], P, -1)

    gu, dn, proj, mrg, wo = [], [], [], [], []
    order = [28, 32, 24, 36]
    for i in range(4):
        order += [40 + i] + ([29 + i, 33 + i, 25 + i, 37 + i] if i < 3 else [12, 13, 14, 15]) + [i, 4 + i, 8 + i]
    for i in range(4):
        order += [16 + i, 20 + i]
    for l in range(DEPTH):
        for f in ("ffn1", "ffn2"):
            g = chunks(a[f + "_w_gate"][l], slice(None))
            u = chunks(a[f + "_w_up"][l], slice(None))
            gu.append(np.stack([g, u], axis=1).reshape(-1, P, D))
            d = blocks(a[f + "_w_down"][l], slice(None)).reshape(KD, P, 2, HALF * P).transpose(0, 2, 1, 3)
            dn.append(d.reshape(-1, P, HALF * P))
        proj.append(chunks(a["w_in"][l], order))
        gates = chunks(a["w_in"][l], slice(44, 68)).reshape(3, KD, P, D)
        for b, name in ((2, "w_branch_c"), (0, "w_branch_a"), (1, "w_branch_b")):
            mrg.append(np.concatenate([gates[b], chunks(a[name][l], slice(None))], axis=2))
        wo.append(chunks(a["w_out"][l], slice(None)))
    per_p = lambda v: v.reshape(DEPTH, -1, P).transpose(2, 0, 1)
    gains = np.concatenate([per_p(a[n]) for n in ("ffn1_norm", "mix_norm", "ffn2_norm", "diff_subln", "hgrn_norm")],
                           axis=2)
    lam_in = np.concatenate([a["diff_lambda_" + n].T for n in ("q1", "k1", "q2", "k2")], axis=1)
    arrays = {
        "xT": a["x"][0].T, "wgu": np.concatenate(gu), "wdn": np.concatenate(dn),
        "wproj": np.concatenate(proj), "wmerge": np.concatenate(mrg), "wout": np.concatenate(wo),
        "gains": gains, "final_g": a["final_norm"].reshape(KD, P).T,
        "lb_raw": per_p(a["hgrn_lower_bounds"]).reshape(P, -1), "lam_in": lam_in,
        "ident": np.eye(P, dtype=np.float32), "masks": level_masks(), "bias": alibi_tables(),
    }
    arrays = {k: np.ascontiguousarray(v) for k, v in arrays.items()}

    nc = bacc.Bacc("TRN2", target_bir_lowering=False, num_devices=1, dynamic_dma_scratch_size=1024)
    aps = [nc.dram_tensor("in_" + k, v.shape, mybir.dt.from_np(v.dtype), kind="ExternalInput").ap()
           for k, v in arrays.items()]
    h_save = nc.dram_tensor("h_save", (D, SEQ), F32, kind="Internal").ap()
    out = nc.dram_tensor("out_T", (D, SEQ), F32, kind="ExternalOutput").ap()
    build(nc, *aps, h_save, out)
    r = run_bass_kernel_spmd(nc, [{"in_" + k: v for k, v in arrays.items()}], core_ids=[0])
    return np.ascontiguousarray(r.results[0]["out_T"].T)[None]
```

```python
import concourse.bass as bass
from concourse import mybir
import numpy as np

F32 = mybir.dt.float32
F32R = mybir.dt.float32r
U8 = mybir.dt.uint8
BF16 = mybir.dt.bfloat16
ALU = mybir.AluOpType
ACT = mybir.ActivationFunctionType
AX = mybir.AxisListType

DEPTH, D, SEQ, DFF = 2, 1024, 512, 2816
P = 128
KD = D // P
KF = DFF // P
TT_ = SEQ // P
HALF = KF // 2
BRK = 512 // P
MB = KD + BRK
SLOT = MB * P
EPS = 1e-6
CS = 64
NC = SEQ // CS
LEVELS = (32, 16, 8, 4, 2, 1)
F_CAP = 43.6
SCALE = 64 ** -0.5
BASE = 1152
UW = 896

GU = (0, 136)
DN = (44, 180)
C_P1 = 60
C_P2, H0 = 64, 3
C_P3 = 96
C_P4 = 112
C_P5 = 120
C_P6 = 128
CH = 196

G_FFN1, G_MIX, G_FFN2, G_SUB, G_HG, LB, OMLB, NLAM, NPAR = 0, 8, 16, 24, 25, 26, 30, 34, 36


def build(nc, xT, wgu, wdn, wproj, wmerge, wout, gains, final_g, lb_raw, lam_in, ident_c, masks_c,
          bias_c, h_save, out):
    from contextlib import ExitStack
    ctx = ExitStack()
    with ctx:
        def at(name, words, offset, dt=F32):
            return nc.alloc_sbuf_tensor_at(name, [P, words], dt, offset=BASE + offset)

        def tiles(t, n=SEQ):
            return t[:, :].rearrange("p (a n) -> p a n", n=n)

        KB = 1024
        raw = tiles(at("raw", 4 * SLOT, 0), SLOT)
        w_hi = tiles(at("w_hi", 2 * SLOT, 24 * KB, F32R), SLOT)
        w_lo = tiles(at("w_lo", 2 * SLOT, 36 * KB, F32R), SLOT)
        x_hi = tiles(at("x_hi", KD * SEQ, 48 * KB, F32R))
        x_lo = tiles(at("x_lo", KD * SEQ, 64 * KB, F32R))
        HB = 80 * KB
        h = tiles(at("h", KD * SEQ, HB))
        ZB = 96 * KB
        zs = lambda s: ZB + 2 * KB * s
        z = tiles(at("z", 52 * SEQ, ZB))
        CB = zs(52)
        SB = CB + 6 * KB
        mask_f = tiles(at("mask_f", len(LEVELS) * P, zs(40)), P)
        act_hi = tiles(at("act_hi", KF * SEQ, zs(0), F32R))
        act_lo = tiles(at("act_lo", KF * SEQ, zs(22), F32R))
        silu_g = tiles(at("silu_g", 2 * SEQ, zs(44)))
        act_f = tiles(at("act_f", 2 * SEQ, zs(46)))
        x_f = tiles(at("x_f", 4 * SEQ, zs(48)))
        h_out = tiles(at("h_out", KD * SEQ, SB))
        h_sq = tiles(at("h_sq", 2 * SEQ, SB + 10 * KB))
        sq_sum = at("sq_sum", SEQ, SB + 14 * KB)
        ya_hi = tiles(at("ya_hi", 4 * SEQ, zs(0), F32R))
        ya_lo = tiles(at("ya_lo", 4 * SEQ, zs(5), F32R))
        yc_hi = tiles(at("yc_hi", 4 * SEQ, zs(10), F32R))
        yc_lo = tiles(at("yc_lo", 4 * SEQ, zs(15), F32R))
        yb_hi = tiles(at("yb_hi", 4 * SEQ, zs(24), F32R))
        yb_lo = tiles(at("yb_lo", 4 * SEQ, zs(28), F32R))
        merged = tiles(at("merged", KD * SEQ, zs(44)))
        m_hi = tiles(at("m_hi", KD * SEQ, zs(32), F32R))
        m_lo = tiles(at("m_lo", KD * SEQ, zs(0), F32R))
        o_f = at("o_f", SEQ, zs(20))
        o_sq = at("o_sq", SEQ, zs(21))
        gate_t = at("gate_t", SEQ, zs(22))
        gated = at("gated", SEQ, zs(23))
        S = at("S", 8 * SEQ, HB)[:, :].rearrange("p (m t n) -> p m t n", m=2, n=SEQ)
        pT_a = tiles(at("pT_a", 4 * SEQ, HB + 8 * KB))
        pT_b = [tiles(at(f"pT_b{m}", 4 * SEQ, zs(10 + 5 * m))) for m in range(2)]
        bias = tiles(at("bias", 2 * UW, SB), UW)
        q_hi = at("q_hi", SEQ, SB + 7 * KB, F32R)
        k_hi = at("k_hi", SEQ, SB + 9 * KB, F32R)
        q_lo = {"a": at("q_lo_a", SEQ, SB + 4 * UW, F32R), "b": at("q_lo_b", SEQ, zs(20), F32R)}
        k_lo = {"a": at("k_lo_a", SEQ, zs(23), F32R), "b": at("k_lo_b", SEQ, zs(21), F32R)}
        v_st = at("v_st", SEQ, SB + 11 * KB)
        v_tok = at("v_tok", SEQ, SB + 13 * KB)
        nf = tiles(at("nf", 2 * SEQ, HB))
        kk = tiles(at("kk", 2 * SEQ, HB + 4 * KB))
        ln1 = tiles(at("ln1", 2 * SEQ, HB + 8 * KB))
        gg = tiles(at("gg", 2 * SEQ, HB + 12 * KB))
        xy = [nf, ln1]
        run = tiles(at("run", 2 * SEQ, zs(36)))
        qk64 = tiles(at("qk64", 4 * SEQ, zs(38)))
        k_sum = at("k_sum", SEQ, zs(42))
        og_t = at("og_t", SEQ, zs(43))
        qkl = [tiles(at(f"qkl{b}", 2 * SEQ, zs(44 + 2 * b))) for b in range(2)]
        q_far = tiles(at("q_far", 6 * P, zs(48)), P)
        hq = at("hq", SEQ, zs(50))
        hi_st = at("hi_st", SEQ, zs(51))
        AT_ = at("AT", 5 * SEQ, SB)
        AT = tiles(AT_)
        ATd = tiles(AT_, SEQ + P)[:, :, 0:P]
        i_tok = at("i_tok", SEQ, SB + 10 * KB)
        ho_f = at("ho_f", SEQ, SB + 12 * KB)
        ho_sq = at("ho_sq", SEQ, SB + 14 * KB)
        ident = at("ident", P, CB)
        ones = at("ones", P, CB + 512)
        masks = tiles(at("masks", len(LEVELS) * SEQ, CB + 1 * KB, U8))
        run_mask = at("run_mask", SEQ, CB + 4 * KB, BF16)
        par2 = at("par2", DEPTH * NPAR, CB + 5 * KB)
        small = at("small", 160, CB + 5 * KB + 320)
        par = small[:, 0:36]
        ms, rt, rs = small[:, 36:40], small[:, 40:44], small[:, 44:48]
        neg_max, p_sum, p_rs, p_c2 = small[:, 48:56], small[:, 56:64], small[:, 64:72], small[:, 72:76]
        lb_h = small[:, 76:78]
        warm = small[:, 78:79]
        tot, ttot = small[:, 80:96], small[:, 96:104]
        fin_g = small[:, 104:112]
        lbr, lbt, lamp = small[:, 112:120], small[:, 120:132], small[:, 132:152]

        bank = [ctx.enter_context(nc.psum_tensor(f"bank{b}", [P, SEQ], F32)) for b in range(8)]

        names = """par_in sq_added const_in lo_done chunk_done prod_taken silu_done act_ready h_upd
            sq_ready xn_odd n_stat n_ms n_rt n_rc n_bc xf_ready xhi_ready xn_ready h_saved h_back out_done
            pre_lam pre_exp par_ready gate_done
            hg_stage hg_it hg_itok hg_nf hg_ln hg_ar hg_kexp hg_rem hg_e hg_q64 hg_q128
            hg_og lv_sub lv_exp lv_mul lev_mm lev_taken od_mm od_taken hg_pv hg_sq hg_st hg_ms
            hg_rt hg_rc hg_bc hg_out out_ready gate_ready m_ready""".split()
        sem = {n: ctx.enter_context(nc.semaphore(n)) for n in names}
        x_in = [ctx.enter_context(nc.semaphore(f"x_in{q}")) for q in range(4)]
        raw_in = [ctx.enter_context(nc.semaphore(f"raw_in{s}")) for s in range(4)]
        att = {b: {n: ctx.enter_context(nc.semaphore(f"{n}_{b}")) for n in
                   "tbl stage qk_split vt vtok sc ttr exp pd tr pt pv osq st ms rt rc bc out".split()} for b in "ab"}
        X = type("Sems", (), sem)


        def loaded(l, base, i, c):
            return ((l * (CH // 4) + i) + ((base + c) // 4 + 1)) * 16

        block = ctx.enter_context(nc.Block())

        @block.sync
        def _(sp):
            for q in range(4):
                sp.dma_start(h[:, 2 * q:2 * q + 2, :], xT.rearrange("(k p) n -> p k n", p=P)[:, 2 * q:2 * q + 2, :])\
                    .then_inc(x_in[q], 16)

            def chunk(l, base, i, c, src, row, words):
                n = l * CH + (base + c) + i * 4
                sp.wait_ge(X.lo_done, n + 1)
                sp.dma_start(raw[:, c, 0:words], src[bass.ds(row, 1), :, :].rearrange("a p n -> (a p) n"))\
                    .then_inc(raw_in[c], 16)

            def ffn(l, s):
                with sp.Fori(0, KF // 2) as i:
                    for c in range(4):
                        chunk(l, GU[s], i, c, wgu, l * 88 + i * 4 + (44 * s + c), D)
                with sp.Fori(0, KD // 2) as i:
                    for c in range(4):
                        chunk(l, DN[s], i, c, wdn, l * 32 + i * 4 + (16 * s + c), HALF * P)

            with sp.Fori(0, DEPTH) as l:
                ffn(l, 0)
                with sp.Fori(0, 9) as i:
                    for c in range(4):
                        chunk(l, C_P1, i, c, wproj, l * 44 + i * 4 + c, D)
                with sp.Fori(0, 4) as i:
                    chunk(l, C_P3, i, 0, wproj, l * 44 + i * 2 + 36, D)
                    chunk(l, C_P3, i, 1, wmerge, l * 24 + i * 2, SLOT)
                    chunk(l, C_P3, i, 2, wproj, l * 44 + i * 2 + 37, D)
                    chunk(l, C_P3, i, 3, wmerge, l * 24 + i * 2 + 1, SLOT)
                with sp.Fori(0, 4) as i:
                    for c in range(4):
                        chunk(l, C_P4, i, c, wmerge, l * 24 + i * 4 + (8 + c), SLOT)
                with sp.Fori(0, 2) as i:
                    for c in range(4):
                        chunk(l, C_P6, i, c, wout, l * 8 + i * 4 + c, D)
                ffn(l, 1)
            for k in range(KD):
                sp.wait_ge(X.out_ready, k + 1)
                sp.dma_start(out[k * P:(k + 1) * P, :], h_out[:, k, :]).then_inc(X.out_done, 16)
            sp.wait_ge(X.out_done, 16 * KD)

        @block.gpsimd
        def _(pool):
            pool.sem_inc(X.lo_done, 4)

            def split(l, base, i, c, words):
                n = l * CH + (base + c) + i * 4
                pool.wait_ge(raw_in[c], loaded(l, base, i, c))
                pool.wait_ge(X.chunk_done, n + 1)
                pool.nop(nofuse=True)
                w, hi, lo = raw[:, c, 0:words], w_hi[:, c % 2, 0:words], w_lo[:, c % 2, 0:words]
                nc.gpsimd.tensor_scalar(hi, w, 1.0, 0.0, ALU.mult, ALU.add)
                pool.drain()
                nc.gpsimd.tensor_tensor(lo, w, hi.bitcast(F32), ALU.subtract).then_inc(X.lo_done, 1)

            def low_halves(nx):
                for k in range(1, KD, 2):
                    pool.wait_ge(X.xhi_ready, nx * KD + (k + 1))
                    pool.nop(nofuse=True)
                    nc.gpsimd.tensor_tensor(x_lo[:, k, :], x_f[:, k % 4, :], x_hi[:, k, :].bitcast(F32), ALU.subtract)\
                        .then_inc(X.xn_odd, 1)

            def first_splits(l, base, nx):
                for c in range(4):
                    if c == 2:
                        low_halves(nx)
                    split(l, base, 0, c, D)

            def ffn(l, s):
                first_splits(l, GU[s], l * 3 + 2 * s)
                with pool.Fori(0, KF // 2 - 1) as i:
                    for c in range(4):
                        split(l, GU[s] + 4, i, c, D)
                with pool.Fori(0, KD // 2) as i:
                    for c in range(4):
                        split(l, DN[s], i, c, HALF * P)

            with pool.Fori(0, DEPTH) as l:
                ffn(l, 0)
                first_splits(l, C_P1, l * 3 + 1)
                with pool.Fori(0, 8) as i:
                    for c in range(4):
                        split(l, C_P1 + 4, i, c, D)
                with pool.Fori(0, 4) as i:
                    for c in range(4):
                        split(l, C_P3, i, c, SLOT if c % 2 else D)
                with pool.Fori(0, 4) as i:
                    for c in range(4):
                        split(l, C_P4, i, c, SLOT)
                with pool.Fori(0, 2) as i:
                    for c in range(4):
                        split(l, C_P6, i, c, D)
                ffn(l, 1)

        @block.tensor
        def _(pe):
            pe.sem_inc(X.chunk_done, 2)
            for b in "ab":
                pe.sem_inc(att[b]["sc"], 1)
            mm = nc.tensor.matmul

            def block_products(dst, c, blocks, xh, xl, start, stop):
                for b, k in blocks:
                    w1, w2 = w_hi[:, c % 2, b * P:(b + 1) * P], w_lo[:, c % 2, b * P:(b + 1) * P]
                    first, last = start and b == blocks[0][0], stop and b == blocks[-1][0]
                    mm(dst[:, :], w1, xh(k), start=first, stop=False)
                    mm(dst[:, :], w1, xl(k), start=False, stop=False)
                    m = mm(dst[:, :], w2, xh(k), start=False, stop=last)
                return m

            def weights(l, base, i, c, lag):
                n = l * CH + (base + c) + i * 4
                pe.wait_ge(X.lo_done, n + 5)
                if lag:
                    pe.wait_ge(X.prod_taken, n + 5 - lag)

            def phase_start(l, base):
                pe.wait_ge(X.prod_taken, l * CH + base + 4)
                pe.nop(nofuse=True)

            xh, xl = (lambda k: x_hi[:, k, :]), (lambda k: x_lo[:, k, :])

            def product(l, base, i, c, dst, lag=4):
                weights(l, base, i, c, lag)
                block_products(dst, c, [(k, k) for k in range(KD)], xh, xl, True, True)\
                    .then_inc(X.chunk_done, 1)

            def first_product(l, base, i, normed):
                weights(l, base, i, 0, 4)
                for k in range(KD):
                    if k % 2:
                        pe.wait_ge(X.xn_odd, normed + (k + 1) // 2)
                    else:
                        pe.wait_ge(X.xn_ready, normed + (k // 2 + 1))
                    m = block_products(bank[0], 0, [(k, k)], xh, xl, k == 0, k == KD - 1)
                m.then_inc(X.chunk_done, 1)

            def gate_product(c, dst):
                return block_products(dst, c, [(k, k) for k in range(KD)], xh, xl, True, True)

            def branch_product(c, dst, yh, yl):
                return block_products(dst, c, [(KD + k, k) for k in range(BRK)],
                                      lambda k: yh[:, k, :], lambda k: yl[:, k, :], True, True)

            def token_sums(sq, dst):
                for t in range(TT_):
                    m = mm(dst[:, t:t + 1], sq[:, t * P:(t + 1) * P], ones[:, 0:1], start=True, stop=True)
                return m

            def spread(dst):
                for t in range(TT_):
                    m = mm(dst[:, t * P:(t + 1) * P], rs[:, t:t + 1].broadcast_to([P, P]), ident[:, :],
                           start=True, stop=True)
                return m

            def norm(nu):
                pe.wait_ge(X.sq_added, nu * KD + KD)
                token_sums(sq_sum, bank[7]).then_inc(X.n_stat, 1)
                pe.wait_ge(X.n_rc, nu + 1)
                spread(bank[6]).then_inc(X.n_bc, 1)

            def ffn(l, s):
                phase_start(l, GU[s])
                with pe.Fori(0, KF // 2) as i:
                    for c in range(4):
                        if c == 0:
                            first_product(l, GU[s], i, l * 12 + 8 * s)
                        else:
                            product(l, GU[s], i, c, bank[c])
                with pe.Fori(0, KD // 2) as i:
                    for c in range(4):
                        weights(l, DN[s], i, c, 0 if c % 2 else 4)
                        pe.wait_ge(X.act_ready, l * 44 + (22 * s + (HALF, KF)[c % 2]))
                        block_products(bank[c - c % 2], c, [(k, (c % 2) * HALF + k) for k in range(HALF)],
                                       lambda k: act_hi[:, k, :], lambda k: act_lo[:, k, :],
                                       c % 2 == 0, c % 2 == 1).then_inc(X.chunk_done, 1)

            def transposes(dst, src):
                for b in range(4):
                    m = nc.tensor.transpose(dst[:, b * P:(b + 1) * P], src[:, b * P:(b + 1) * P], ident[:, :])
                return m

            def v_to_tokens(a, u):
                pe.wait_ge(a["out"], u + 1)
                pe.wait_ge(a["stage"], u + 1)
                transposes(bank[6], v_st).then_inc(a["vt"], 1)
                pe.wait_ge(a["qk_split"], u + 1)

            def scores(b, u, query_tiles):
                a = att[b]
                for t in query_tiles:
                    if t == 1:
                        pe.wait_ge(a["vtok"], u + 1)
                    if t >= 2:
                        pe.wait_ge(a["ttr"], u * 8 + (2 * t - 2) + 1)
                    q = slice(t * P, (t + 1) * P)
                    for n, (lhs, rhs) in enumerate(((q_hi, k_hi), (q_hi, k_lo[b]), (q_lo[b], k_hi))):
                        for m in range(2):
                            r = slice(64 * m, 64 * m + 64)
                            x = mm(bank[4 + 2 * (t % 2) + m][:, :], lhs[r, q], rhs[r, :], start=(n == 0), stop=(n == 2))
                            if n == 2:
                                x.then_inc(a["sc"], 1)

            pe.wait_ge(X.const_in, 32)
            pe.wait_ge(X.pre_lam, 1)
            mm(bank[5][:, 0:4], ones[0:64, :], lamp[0:64, 8:12], start=True, stop=True).then_inc(X.pre_exp, 1)

            with pe.Fori(0, DEPTH) as l:
                norm(l * 3)
                ffn(l, 0)
                norm(l * 3 + 1)
                phase_start(l, C_P1)
                first_product(l, C_P1, 0, l * 12 + 4)
                for c in range(1, 7):
                    product(l, C_P1, 0, c, bank[c % 4])
                sl = lambda t: slice(t * P, (t + 1) * P)

                def level(u, n, lhs, rhs):
                    pe.wait_ge(X.lev_taken, u * 8 + (n + 1))
                    b = bank[4 + n % 2]
                    for t in range(TT_):
                        m = mm(b[:, sl(t)], lhs[:, sl(t)], rhs[:, sl(t)], start=True, stop=True)
                    m.then_inc(X.lev_mm, 1)

                def head(i, last):
                    u = l * 4 + i
                    pe.wait_ge(X.hg_stage, u + 1)
                    transposes(bank[6], hi_st).then_inc(X.hg_it, 1)
                    pe.wait_ge(X.hg_q64, u + 1)
                    level(u, 0, k_sum, hq)
                    pe.wait_ge(X.lev_taken, u * 8 + 2)
                    for t in range(TT_):
                        a, b = slice(t * P, t * P + CS), slice(t * P + CS, (t + 1) * P)
                        mm(bank[5][0:CS, b], qk64[:, 2, a], qk64[:, 0, b], start=True, stop=True)
                        m = mm(bank[5][CS:P, a], qk64[:, 3, b], qk64[:, 1, a], start=True, stop=True)
                    m.then_inc(X.lev_mm, 1)
                    product(l, C_P2, i * 2, H0 + 0, bank[3])
                    pe.wait_ge(X.hg_q128, u + 1)
                    pe.wait_ge(X.hg_itok, u + 1)
                    pe.wait_ge(X.hg_out, u + 1)
                    far = {(0, 2): 0, (1, 3): 1, (0, 3): 2, (3, 1): 3, (2, 0): 4, (3, 0): 5}
                    for a in range(4):
                        if a >= 2:
                            pe.wait_ge(X.od_taken, u * 4 + (a - 1))
                        for b in range(4):
                            if a != b:
                                rhs = q_far[:, far[a, b], :] if (a, b) in far else qk64[:, int(a > b), sl(b)]
                                m = mm(bank[6 + a % 2][:, sl(b)], qk64[:, 2 + int(a > b), sl(a)], rhs,
                                       start=True, stop=True)
                        m.then_inc(X.od_mm, 1)
                        if a == 1:
                            product(l, C_P2, i * 2, H0 + 1, bank[0])
                    for j in range(len(LEVELS)):
                        pe.wait_ge(X.lv_mul, u * 6 + (j + 1) + 1)
                        level(u, j + 2, qkl[j % 2][:, 1, :], qkl[j % 2][:, 0, :])
                        if j in ((1, 3) if last else (1, 2, 4)):
                            c = H0 + {1: 2, 2: 3, 3: 3, 4: 4}[j]
                            product(l, C_P2, i * 2, c, bank[c % 4])
                    pe.wait_ge(X.od_taken, u * 4 + 4)
                    pe.wait_ge(X.lev_taken, u * 8 + 10)
                    for a in range(4):
                        m = mm(bank[6][:, :], i_tok[:, sl(a)], AT[:, a, :], start=(a == 0), stop=(a == 3))
                    m.then_inc(X.hg_pv, 1)
                    if not last:
                        product(l, C_P2, i * 2, H0 + 5, bank[0])
                    pe.wait_ge(X.hg_sq, u + 1)
                    token_sums(ho_sq, bank[7]).then_inc(X.hg_st, 1)
                    for c in [H0 + 4] if last else [H0 + 6, H0 + 7]:
                        product(l, C_P2, i * 2, c, bank[c % 4])
                    pe.wait_ge(X.hg_rc, u + 1)
                    spread(bank[7]).then_inc(X.hg_bc, 1)
                with pe.Fori(0, 3) as i:
                    head(i, False)
                head(3, True)
                A = att["a"]
                with pe.Fori(0, 4) as i:
                    u = l * 4 + i
                    product(l, C_P3, i, 0, bank[0], lag=2)
                    v_to_tokens(A, u)
                    scores("a", u, (0, 1))
                    weights(l, C_P3, i, 1, 2)
                    pe.wait_ge(X.hg_out, l * 4 + 4 + 1)
                    branch_product(1, bank[3], yc_hi, yc_lo)
                    scores("a", u, (2, 3))
                    gate_product(1, bank[2]).then_inc(X.chunk_done, 1)
                    pe.wait_ge(A["vtok"], u + 1)
                    for t in range(TT_):
                        pe.wait_ge(A["pd"], u * 4 + (t + 1))
                        if t >= 2:
                            pe.wait_ge(A["pt"], u * 4 + (t - 1))
                        transposes(bank[6 + t % 2], S[:, 0, t, :]).then_inc(A["tr"], 1)
                    product(l, C_P3, i, 2, bank[1], lag=2)
                    pe.wait_ge(A["pt"], u * 4 + 4)
                    for k in range(TT_):
                        m = mm(bank[4][:, :].rearrange("p (t n) -> p t n", n=P), v_tok[:, k * P:(k + 1) * P],
                               pT_a[:, :, k * P:(k + 1) * P],
                               start=(k == 0), stop=(k == TT_ - 1))
                    m.then_inc(A["pv"], 1)
                    weights(l, C_P3, i, 3, 2)
                    gate_product(3, bank[2])
                    pe.wait_ge(A["osq"], u + 1)
                    token_sums(o_sq, bank[5]).then_inc(A["st"], 1)
                    branch_product(3, bank[3], yc_hi, yc_lo).then_inc(X.chunk_done, 1)
                    pe.wait_ge(A["rc"], u + 1)
                    spread(bank[7]).then_inc(A["bc"], 1)
                B = att["b"]
                with pe.Fori(0, 2) as i:
                    for r in range(2):
                        u = l * 4 + i * 2 + r
                        weights(l, C_P4, i, 2 * r, 2)
                        gate_product(2 * r, bank[0])
                        v_to_tokens(B, u)
                        scores("b", u, (0, 1))
                        pe.wait_ge(A["out"], l * 4 + 4 + 1)
                        branch_product(2 * r, bank[1], ya_hi, ya_lo).then_inc(X.chunk_done, 1)
                        scores("b", u, (2, 3))
                        weights(l, C_P4, i, 2 * r + 1, 2)
                        gate_product(2 * r + 1, bank[2])
                        pe.wait_ge(B["vtok"], u + 1)
                        for g in range(8):
                            pe.wait_ge(B["pd"], u * 8 + (g + 1))
                            if g >= 2:
                                pe.wait_ge(B["pt"], u * 8 + (g - 1))
                            transposes(bank[6 + g % 2], S[:, g // 4, g % 4, :]).then_inc(B["tr"], 1)
                            if g == 5:
                                branch_product(2 * r + 1, bank[3], ya_hi, ya_lo).then_inc(X.chunk_done, 1)
                        for m_ in range(2):
                            pe.wait_ge(B["pt"], u * 8 + 4 * (m_ + 1))
                            for k in range(TT_):
                                m = mm(bank[4][64 * m_:64 * m_ + 64, :],
                                       v_tok[:, k * P + 64 * m_:k * P + 64 * m_ + 64], pT_b[m_][:, k, :],
                                       start=(k == 0), stop=(k == TT_ - 1))
                        m.then_inc(B["pv"], 1)
                with pe.Fori(0, 2) as i:
                    for c in range(4):
                        weights(l, C_P5, i, c, 2)
                        gate_product(c, bank[2 * (c % 2)])
                        pe.wait_ge(B["out"], l * 4 + 4 + 1)
                        branch_product(c, bank[2 * (c % 2) + 1], yb_hi, yb_lo).then_inc(X.chunk_done, 1)
                with pe.Fori(0, 2) as i:
                    for c in range(4):
                        weights(l, C_P6, i, c, (2, 4, 3, 4)[c])
                        for k in range(KD):
                            pe.wait_ge(X.m_ready, l * KD + (k + 1))
                            m = block_products(bank[c], c, [(k, k)], lambda k: m_hi[:, k, :],
                                               lambda k: m_lo[:, k, :], k == 0, k == KD - 1)
                        m.then_inc(X.chunk_done, 1)
                norm(l * 3 + 2)
                ffn(l, 1)
            norm(DEPTH * 3)

        @block.scalar
        def _(act):
            A_ = nc.scalar.activation
            act.dma_start(par2[:, :].rearrange("p (l c) -> p l c", l=DEPTH)[:, :, 0:26], gains[:, :, :])\
                .then_inc(X.par_in, 16)
            act.dma_start(lbr, lb_raw[:, :]).then_inc(X.par_in, 16)
            act.dma_start(lamp[0:64, 0:8], lam_in[:, :]).then_inc(X.par_in, 16)
            act.dma_start(small[:, 104:112], final_g[:, :]).then_inc(X.par_in, 16)
            act.dma_start(ident[:, :], ident_c[:, :]).then_inc(X.const_in, 16)
            act.dma_start(mask_f[:, :, :], masks_c.rearrange("p (j n) -> p j n", n=P)).then_inc(X.const_in, 16)
            def squares(nu):
                for k in range(KD):
                    act.wait_ge(X.h_upd, nu * KD + (k + 1))
                    if k >= 2:
                        act.wait_ge(X.sq_added, nu * KD + (k - 1))
                    A_(h_sq[:, k % 2, :], h[:, k, :], ACT.Square).then_inc(X.sq_ready, 1)

            def root(nu):
                A_(warm, ones[:, 0:1], ACT.Sqrt)
                act.wait_ge(X.n_ms, nu + 1)
                A_(rt, ms, ACT.Sqrt).then_inc(X.n_rt, 1)

            def halves(nx):
                for k in range(KD):
                    act.wait_ge(X.xf_ready, nx * KD + (k + 1))
                    A_(x_hi[:, k, :], x_f[:, k % 4, :], ACT.Copy).then_inc(X.xhi_ready, 1)

            def ffn(l, s):
                with act.Fori(0, KF // 2) as i:
                    for v in range(2):
                        n = l * CH + (GU[s] + 2 * v) + i * 4
                        act.wait_ge(X.chunk_done, n + 3)
                        act.wait_ge(X.prod_taken, n + 2)
                        A_(silu_g[:, v, :], bank[2 * v][:, :], ACT.Silu).then_inc(X.silu_done, 1)

            def take(l, base, i, c, slot):
                n = l * CH + (base + c) + i * 4
                act.wait_ge(X.chunk_done, n + 3)
                act.nop(nofuse=True)
                A_(z[:, bass.ds(slot, 1), :].rearrange("p a n -> p (a n)"), bank[c % 4][:, :], ACT.Copy)\
                    .then_inc(X.prod_taken, 1)

            def gate(l, base, i, c, b, count):
                n = l * CH + (base + c) + i * 4
                act.wait_ge(X.chunk_done, n + 3)
                act.wait_ge(X.gate_done, count + 1)
                A_(gate_t[:, :], bank[b][:, :], ACT.Tanh, scale=0.5).then_inc(X.gate_ready, 1)

            def stage(dst, slot):
                return A_(dst[:, :], z[:, bass.ds(slot, 1), :].rearrange("p a n -> p (a n)"), ACT.Copy)

            def attention_in(a, u, tables, qkv):
                act.wait_ge(a["ttr"], u * 8 + 1)
                for m, row in enumerate(tables):
                    act.dma_start(bias[:, m, :], bias_c[bass.ds(row, 1), :, :].rearrange("a p n -> (a p) n"))\
                        .then_inc(a["tbl"], 16)
                act.wait_ge(a["sc"], u * 8 + 1)
                act.nop(nofuse=True)
                for dst, slot in zip((q_hi, k_hi, v_st), qkv):
                    stage(dst, slot)
                act.drain().then_inc(a["stage"], 1)
                act.wait_ge(a["vt"], u + 1)
                A_(v_tok[:, :], bank[6][:, :], ACT.Copy).then_inc(a["vtok"], 1)
                for g in range(8):
                    act.wait_ge(a["ttr"], u * 8 + (g + 1) + 1)
                    t, m = divmod(g, 2)
                    col = slice(4 * m + t, 4 * m + t + 1)
                    A_(S[:, m, t, :], S[:, m, t, :], ACT.Exp, bias=neg_max[:, col],
                       scale=-1.0, accum_out=p_sum[:, col]).then_inc(a["exp"], 1)

            def p_columns(a, u, n, g, dst):
                t = g % 4
                act.wait_ge(a["tr"], u * n + (g + 1))
                A_(dst[:, :, t * P:(t + 1) * P], bank[6 + g % 2][:, :].rearrange("p (k n) -> p k n", n=P),
                   ACT.Copy).then_inc(a["pt"], 1)

            squares(0)
            act.wait_ge(X.pre_exp, 1)
            act.wait_ge(X.pre_lam, 2)
            A_(lamp[:, 12:16], bank[5][:, 0:4], ACT.Exp)
            A_(lbt[:, 0:8], lbr, ACT.Exp)
            act.drain().then_inc(X.pre_exp, 1)

            with act.Fori(0, DEPTH) as l:
                root(l * 3)
                halves(l * 3)
                ffn(l, 0)
                squares(l * 3 + 1)
                root(l * 3 + 1)
                halves(l * 3 + 1)
                act.wait_ge(X.xn_ready, l * 12 + 8)
                act.wait_ge(X.xf_ready, l * 24 + 16)
                act.dma_start(h_save.rearrange("(k p) n -> p k n", p=P), h[:, :, :]).then_inc(X.h_saved, 16)
                def lv(u, j):
                    act.wait_ge(X.lv_sub, u * 6 + (j + 1))
                    A_(xy[j % 2][:, :, :], xy[j % 2][:, :, :], ACT.Exp).then_inc(X.lv_exp, 1)

                def head_logs(u):
                    act.wait_ge(X.hg_nf, u + 1)
                    A_(kk[:, :, :], nf[:, :, :], ACT.Exp)
                    act.drain()
                    A_(ln1[:, :, :], kk[:, :, :], ACT.Ln, bias=1.0)
                    A_(gg[:, :, :], kk[:, :, :], ACT.Ln, bias=1.0, scale=lb_h[:, 0:1])
                    act.drain().then_inc(X.hg_ln, 1)

                def head_stage(i, u, taken):
                    act.wait_ge(X.prod_taken, taken)
                    act.wait_ge(X.lv_mul, u * 6 + 1)
                    act.nop(nofuse=True)
                    stage(hq, i + 10)
                    stage(hi_st, i + 15)
                    act.drain().then_inc(X.hg_stage, 1)

                def head_exps(u):
                    act.wait_ge(X.hg_ar, u + 1)
                    A_(kk[:, :, :], nf[:, :, :], ACT.Exp).then_inc(X.hg_kexp, 1)
                    act.wait_ge(X.hg_rem, u + 1)
                    A_(qk64[:, 0:2, :], run[:, :, :], ACT.Exp)
                    A_(qk64[:, 2:4, :], qk64[:, 2:4, :], ACT.Exp)
                    act.drain().then_inc(X.hg_e, 1)
                    lv(u, 0)
                    lv(u, 1)

                def head(i, last):
                    u = l * 4 + i
                    act.wait_ge(X.hg_it, u + 1)
                    A_(i_tok[:, :], bank[6][:, :], ACT.Copy).then_inc(X.hg_itok, 1)
                    take(l, C_P2, i * 2, H0 + 0, i + 1)
                    for a in range(4):
                        if a == 2:
                            take(l, C_P2, i * 2, H0 + 1, i + 6)
                        act.wait_ge(X.od_mm, u * 4 + (a + 1))
                        for lo_, hi_ in ((0, a), (a + 1, 4)):
                            if hi_ > lo_:
                                A_(AT[:, a, lo_ * P:hi_ * P], bank[6 + a % 2][:, lo_ * P:hi_ * P], ACT.Copy)
                        act.drain().then_inc(X.od_taken, 1)
                    lv(u, 2)
                    lv(u, 3)
                    take(l, C_P2, i * 2, H0 + 2, i + 11)
                    lv(u, 4)
                    if not last:
                        take(l, C_P2, i * 2, H0 + 3, i + 16)
                    lv(u, 5)
                    if last:
                        take(l, C_P2, i * 2, H0 + 3, i + 16)
                    act.wait_ge(X.hg_out, u + 1)
                    act.nop(nofuse=True)
                    A_(og_t[:, :], z[:, bass.ds(i + 20, 1), :].rearrange("p a n -> p (a n)"), ACT.Tanh, scale=0.5)\
                        .then_inc(X.hg_og, 1)
                    if not last:
                        take(l, C_P2, i * 2, H0 + 4, i + 21)
                        head_logs(u + 1)
                        head_stage(i + 1, u + 1, l * CH + (C_P2 + H0 + 4 + 4) + i * 8)
                    act.wait_ge(X.hg_pv, u + 1)
                    A_(ho_sq[:, :], bank[6][:, :], ACT.Square)
                    A_(ho_f[:, :], bank[6][:, :], ACT.Copy)
                    act.drain().then_inc(X.hg_sq, 1)
                    if last:
                        A_(warm, ones[:, 0:1], ACT.Sqrt)
                    if not last:
                        head_exps(u + 1)
                        take(l, C_P2, i * 2, H0 + 5, i + 25)
                    act.wait_ge(X.hg_ms, u + 1)
                    A_(rt, ms, ACT.Sqrt).then_inc(X.hg_rt, 1)
                    if last:
                        take(l, C_P2, i * 2, H0 + 4, i + 32)
                    else:
                        take(l, C_P2, i * 2, H0 + 6, i + 29)
                        take(l, C_P2, i * 2, H0 + 7, i + 32)

                take(l, C_P1, 0, 0, 0)
                take(l, C_P1, 0, 1, 5)
                head_logs(l * 4)
                take(l, C_P1, 0, 2, 10)
                take(l, C_P1, 0, 3, 15)
                head_stage(0, l * 4, l * CH + (C_P1 + 4 + 4))
                head_exps(l * 4)
                for c in range(4, 7):
                    take(l, C_P1, 0, c, 20 + 4 * (c - 4))
                with act.Fori(0, 3) as i:
                    head(i, False)
                head(3, True)
                A = att["a"]
                act.wait_ge(X.hg_out, l * 4 + 4 + 1)
                act.wait_ge(X.prod_taken, l * CH + (C_P3 + 4))
                act.nop(nofuse=True)
                with act.Fori(0, 4) as i:
                    u = l * 4 + i
                    attention_in(A, u, [i], (i + 24, i + 28, i + 32))
                    gate(l, C_P3, i, 1, 2, l * 24 + i * 2)
                    for t in range(TT_):
                        act.wait_ge(A["tr"], u * 4 + (t + 1))
                        A_(pT_a[:, t, :], bank[6 + t % 2][:, :], ACT.Copy).then_inc(A["pt"], 1)
                    act.wait_ge(A["pv"], u + 1)
                    A_(o_sq[:, :], bank[4][:, :], ACT.Square)
                    A_(o_f[:, :], bank[4][:, :], ACT.Copy)
                    act.drain().then_inc(A["osq"], 1)
                    A_(warm, ones[:, 0:1], ACT.Sqrt)
                    act.wait_ge(A["ms"], u + 1)
                    A_(rt, ms, ACT.Sqrt).then_inc(A["rt"], 1)
                    gate(l, C_P3, i, 3, 2, l * 24 + i * 2 + 1)
                B = att["b"]
                act.wait_ge(X.prod_taken, l * CH + (C_P4 - 1 + 4))
                act.nop(nofuse=True)
                with act.Fori(0, 2) as i:
                    for r in range(2):
                        u = l * 4 + i * 2 + r
                        p = i * 2 + r
                        attention_in(B, u, [i * 4 + (4 + 2 * r), i * 4 + (5 + 2 * r)],
                                     (p * 5 + 4, p + 36, p + 40))
                        gate(l, C_P4, i, 2 * r, 0, l * 24 + i * 4 + (8 + 2 * r))
                        for g in range(8):
                            p_columns(B, u, 8, g, pT_b[g // 4])
                        gate(l, C_P4, i, 2 * r + 1, 2, l * 24 + i * 4 + (9 + 2 * r))
                act.wait_ge(B["out"], l * 4 + 4 + 1)
                act.wait_ge(X.h_saved, l * 16 + 16)
                act.dma_start(h[:, :, :], h_save.rearrange("(k p) n -> p k n", p=P)).then_inc(X.h_back, 16)
                with act.Fori(0, 2) as i:
                    for c in range(4):
                        gate(l, C_P5, i, c, 2 * (c % 2), l * 24 + i * 4 + (16 + c))
                squares(l * 3 + 2)
                root(l * 3 + 2)
                halves(l * 3 + 2)
                ffn(l, 1)
                squares(l * 3 + 3)
            root(DEPTH * 3)

        @block.vector
        def _(dve):
            V = nc.vector
            dve.sem_inc(X.prod_taken, 4)
            dve.sem_inc(X.lev_taken, 2)
            for s in (X.hg_out, X.lv_mul, X.gate_done, att["a"]["ttr"], att["a"]["out"], att["b"]["ttr"], att["b"]["out"]):
                dve.sem_inc(s, 1)
            V.memset(ones[:, :], 1.0)
            V.memset(run_mask[:, :], 1.0)
            V.memset(sq_sum[:, :], 0.0)
            dve.drain()

            def add_square(v, tile):
                dve.wait_ge(X.sq_ready, tile + 1)
                V.tensor_tensor(sq_sum[:, :], h_sq[:, v, :], sq_sum[:, :], ALU.add)
                dve.drain().then_inc(X.sq_added, 1)

            for k in range(KD):
                if k % 2 == 0:
                    dve.wait_ge(x_in[k // 2], 16)
                    dve.sem_inc(X.h_upd, 2)
                add_square(k % 2, k)
            dve.wait_ge(X.par_in, 64)
            V.tensor_tensor(lamp[0:64, 8:10], lamp[0:64, 0:2], lamp[0:64, 2:4], ALU.mult)
            V.tensor_tensor(lamp[0:64, 10:12], lamp[0:64, 4:6], lamp[0:64, 6:8], ALU.mult)
            dve.drain().then_inc(X.pre_lam, 1)
            V.memset(run_mask[:, :].rearrange("p (c t) -> p c t", t=CS)[:, :, 0:1], 0.0)
            V.tensor_tensor(lbt[:, 8:12], lbr[:, 0:4], lbr[:, 4:8], ALU.max)
            dve.drain()
            V.tensor_tensor(lbr[:, 0:4], lbr[:, 0:4], lbt[:, 8:12], ALU.subtract)
            V.tensor_tensor(lbr[:, 4:8], lbr[:, 4:8], lbt[:, 8:12], ALU.subtract)
            dve.drain().then_inc(X.pre_lam, 1)
            dve.wait_ge(X.const_in, 32)
            V.tensor_copy(masks[:, :, :].rearrange("p j (a n) -> p j a n", n=P),
                          mask_f[:, :, :].rearrange("p j (a n) -> p j a n", a=1)
                          .broadcast_to([P, len(LEVELS), TT_, P]))
            dve.wait_ge(X.pre_exp, 2)
            V.tensor_tensor(lbt[:, 8:12], lbt[:, 0:4], lbt[:, 4:8], ALU.add)
            V.tensor_tensor(lamp[:, 16:18], lamp[:, 14:16], lamp[:, 12:14], ALU.subtract)
            dve.drain()
            V.reciprocal(lbt[:, 8:12], lbt[:, 8:12])
            dve.drain()
            for l in range(DEPTH):
                p0 = l * NPAR
                lam_init = 0.8 - 0.6 * float(np.exp(-0.3 * l))
                if l == 0:
                    V.memset(par2[:, p0 + LB:p0 + LB + 4], 0.0)
                else:
                    V.tensor_tensor(par2[:, p0 + LB:p0 + LB + 4], lbt[:, 4:8], lbt[:, 8:12], ALU.mult)
                V.tensor_scalar(par2[:, p0 + NLAM:p0 + NLAM + 1], lamp[:, 16 + l:17 + l], -lam_init, None, ALU.add)
                V.tensor_scalar(par2[:, p0 + G_SUB:p0 + G_SUB + 1], par2[:, p0 + G_SUB:p0 + G_SUB + 1],
                                1.0 - lam_init, None, ALU.mult)
                V.tensor_scalar(par2[:, p0 + G_HG:p0 + G_HG + 1], par2[:, p0 + G_HG:p0 + G_HG + 1],
                                0.5, None, ALU.mult)
            dve.drain()
            for l in range(DEPTH):
                p0 = l * NPAR
                V.tensor_scalar(par2[:, p0 + OMLB:p0 + OMLB + 4], par2[:, p0 + LB:p0 + LB + 4],
                                -1.0, 1.0, ALU.mult, ALU.add)
            V.memset(par2[:, NLAM + 1:NLAM + 2], 0.0)
            V.memset(par2[:, NPAR + NLAM + 1:NPAR + NLAM + 2], 0.0)
            dve.drain()
            def inverse_rms(width, stat, done_ms, rt_in, done_rc, nu, ready):
                dve.wait_ge(ready, nu + 1)
                V.tensor_scalar(ms, stat[:, 0:4], 1.0 / width, EPS, ALU.mult, ALU.add).then_inc(done_ms, 1)
                dve.wait_ge(rt_in, nu + 1)
                V.reciprocal(rs, rt).then_inc(done_rc, 1)

            def norm(nu, g0):
                inverse_rms(D, bank[7], X.n_ms, X.n_rt, X.n_rc, nu, X.n_stat)
                dve.wait_ge(X.n_bc, nu + 1)
                for k in range(KD + 1):
                    if k < KD:
                        if k in (5, 7):
                            dve.wait_ge(X.xn_odd, nu * 4 + (k - 3) // 2)
                        V.scalar_tensor_tensor(x_f[:, k % 4, :], h[:, k, :], par[:, g0 + k:g0 + k + 1],
                                               bank[6][:, :], ALU.mult, ALU.mult).then_inc(X.xf_ready, 1)
                    if k % 2:
                        dve.wait_ge(X.xhi_ready, nu * KD + k)
                        V.tensor_tensor(x_lo[:, k - 1, :], x_f[:, (k - 1) % 4, :],
                                        x_hi[:, k - 1, :].bitcast(F32), ALU.subtract)
                        dve.drain().then_inc(X.xn_ready, 1)

            def ffn(l, s):
                with dve.Fori(0, KF // 2) as i:
                    for v in range(2):
                        n = l * CH + (GU[s] + 2 * v + 1) + i * 4
                        f = i * 2 + v
                        dve.wait_ge(X.chunk_done, n + 3)
                        dve.wait_ge(X.silu_done, l * 44 + i * 2 + (22 * s + v + 1))
                        V.tensor_tensor(act_f[:, v, :], silu_g[:, v, :], bank[2 * v + 1][:, :], ALU.mult)
                        dve.drain().then_inc(X.prod_taken, 2)
                        hi = act_hi[:, bass.ds(f, 1), :].rearrange("p a n -> p (a n)")
                        lo = act_lo[:, bass.ds(f, 1), :].rearrange("p a n -> p (a n)")
                        V.tensor_copy(hi, act_f[:, v, :])
                        dve.drain()
                        V.tensor_tensor(lo, act_f[:, v, :], hi.bitcast(F32), ALU.subtract)
                        dve.drain().then_inc(X.act_ready, 1)
                V.memset(sq_sum[:, :], 0.0)
                dve.drain()
                with dve.Fori(0, KD // 2) as i:
                    for v in range(2):
                        n = l * CH + (DN[s] + 2 * v + 1) + i * 4
                        dve.wait_ge(X.chunk_done, n + 3)
                        hj = h[:, bass.ds(i * 2 + v, 1), :].rearrange("p a n -> p (a n)")
                        V.scalar_tensor_tensor(hj, bank[2 * v][:, :], 0.5, hj, ALU.mult, ALU.add)\
                            .then_inc(X.h_upd, 1)
                        dve.drain().then_inc(X.prod_taken, 2)
                        add_square(v, l * 24 + i * 2 + (8 + 16 * s + v))

            def take(l, base, i, c, b, slot):
                n = l * CH + (base + c) + i * 4
                dve.wait_ge(X.chunk_done, n + 3)
                dve.nop(nofuse=True)
                V.tensor_copy(z[:, bass.ds(slot, 1), :].rearrange("p a n -> p (a n)"), bank[b][:, :])\
                    .then_inc(X.prod_taken, 1)

            def gated_sum(l, base, i, c, b, count, j, how):
                dve.wait_ge(X.gate_ready, count + 1)
                dve.wait_ge(X.chunk_done, l * CH + (base + c + 3) + i * 4)
                mj = merged[:, bass.ds(j, 1), :].rearrange("p a n -> p (a n)")
                dst = mj if how == "first" else gated[:, :]
                V.scalar_tensor_tensor(dst, gate_t[:, :], 1.0, bank[b][:, :], ALU.add, ALU.mult)
                dve.drain().then_inc(X.prod_taken, 1)
                if how == "first":
                    dve.sem_inc(X.gate_done, 1)
                    return
                V.tensor_tensor(mj if how == "more" else gated[:, :], gated[:, :], mj, ALU.add)
                dve.drain().then_inc(X.gate_done, 1)
                if how == "last":
                    mh = m_hi[:, bass.ds(j, 1), :].rearrange("p a n -> p (a n)")
                    ml = m_lo[:, bass.ds(j, 1), :].rearrange("p a n -> p (a n)")
                    V.tensor_scalar(mh, gated[:, :], 0.5, None, ALU.mult)
                    dve.drain()
                    V.scalar_tensor_tensor(ml, gated[:, :], 0.5, mh.bitcast(F32), ALU.mult, ALU.subtract)
                    dve.drain().then_inc(X.m_ready, 1)

            def row_max(b, u, tables, slots):
                a = att[b]
                dve.wait_ge(a["stage"], u + 1)
                dve.nop(nofuse=True)
                V.tensor_tensor(q_lo[b][:, :], tile_of(z, slots[0]), q_hi[:, :].bitcast(F32), ALU.subtract)
                V.tensor_tensor(k_lo[b][:, :], tile_of(z, slots[1]), k_hi[:, :].bitcast(F32), ALU.subtract)
                dve.drain().then_inc(a["qk_split"], 1)
                dve.wait_ge(a["tbl"], (u + 1) * (16 * tables))
                for g in range(8):
                    t, m = divmod(g, 2)
                    dve.wait_ge(a["sc"], u * 8 + (g + 1) + 1)
                    dve.nop(nofuse=True)
                    V.tensor_tensor_reduce(out=S[:, m, t, :], in0=bank[4 + 2 * (t % 2) + m][:, :],
                                           in1=bias[:, m if tables == 2 else 0, 384 - t * P:384 - t * P + SEQ],
                                           scale=-SCALE, scalar=3.0e38, op0=ALU.add, op1=ALU.min,
                                           accum_out=neg_max[:, 4 * m + t:4 * m + t + 1])
                    dve.drain().then_inc(a["ttr"], 1)
                dve.wait_ge(a["exp"], u * 8 + 8)
                V.reciprocal(p_rs, p_sum)
                dve.drain()

            def split(hi, lo, src):
                V.tensor_copy(hi, src)
                dve.drain()
                V.tensor_tensor(lo, src, hi.bitcast(F32), ALU.subtract)

            tile_of = lambda t, j: t[:, bass.ds(j, 1), :].rearrange("p a n -> p (a n)")

            with dve.Fori(0, DEPTH) as l:
                V.tensor_copy(par, par2[:, bass.ds(l * NPAR, NPAR)])
                dve.drain()
                norm(l * 3, G_FFN1)
                ffn(l, 0)
                norm(l * 3 + 1, G_MIX)
                dve.wait_ge(X.h_saved, l * 16 + 16)
                dve.nop(nofuse=True)
                rc = lambda t: t.rearrange("p (c t) -> p c t", t=CS)
                sl = lambda t: slice(t * P, (t + 1) * P)

                def halves_of(t, m):
                    return t.rearrange("p (b s m) -> p b s m", s=2, m=m)

                def level_sub(j):
                    m = LEVELS[j]
                    nb = SEQ // (2 * m)
                    x, y = halves_of(xy[j % 2][:, 0, :], m), halves_of(xy[j % 2][:, 1, :], m)
                    rf, rb = halves_of(run[:, 0, :], m), halves_of(run[:, 1, :], m)
                    cf = rf[:, :, 0, m - 1:m].broadcast_to([P, nb, m])
                    cb = rb[:, :, 1, 0:1].broadcast_to([P, nb, m])
                    V.tensor_tensor(x[:, :, 1, :], rf[:, :, 1, :], cf, ALU.subtract)
                    V.tensor_tensor(y[:, :, 0, :], cf, rf[:, :, 0, :], ALU.subtract)
                    V.tensor_tensor(x[:, :, 0, :], rb[:, :, 0, :], cb, ALU.subtract)
                    V.tensor_tensor(y[:, :, 1, :], cb, rb[:, :, 1, :], ALU.subtract)
                    dve.drain().then_inc(X.lv_sub, 1)

                def level_mul(u, j):
                    m = LEVELS[j]
                    dve.wait_ge(X.lv_exp, u * 6 + (j + 1))
                    dve.wait_ge(X.lev_mm, u * 8 + (j + 1))
                    e, o = xy[j % 2], qkl[j % 2]
                    V.tensor_tensor(o[:, 0, :], e[:, 0, :], hq[:, :], ALU.mult)
                    for s in range(2):
                        V.tensor_tensor(halves_of(o[:, 1, :], m)[:, :, s, :], halves_of(e[:, 1, :], m)[:, :, s, :],
                                        halves_of(kk[:, s, :], m)[:, :, s, :], ALU.mult)
                    dve.drain().then_inc(X.lv_mul, 1)

                def level_take(u, j):
                    dve.wait_ge(X.lev_mm, u * 8 + (j + 3))
                    dve.nop(nofuse=True)
                    V.copy_predicated(ATd, masks[:, j, :].rearrange("p (a n) -> p a n", n=P),
                                      bank[4 + j % 2][:, :].rearrange("p (a n) -> p a n", n=P))
                    dve.drain().then_inc(X.lev_taken, 1)

                def head_gates(i, u, taken):
                    dve.wait_ge(X.prod_taken, taken)
                    dve.nop(nofuse=True)
                    f2 = z[:, 0:10, :].rearrange("p (d a) n -> p d a n", d=2)[:, :, bass.ds(i, 1), :]\
                        .rearrange("p d a n -> p d (a n)")
                    V.tensor_copy(lb_h[:, 0:1], par[:, bass.ds(i + LB, 1)])
                    V.tensor_copy(lb_h[:, 1:2], par[:, bass.ds(i + OMLB, 1)])
                    V.tensor_scalar(nf[:, :, :], f2, -1.0, F_CAP, ALU.mult, ALU.min)
                    dve.drain().then_inc(X.hg_nf, 1)
                    dve.wait_ge(X.hg_ln, u + 1)
                    V.tensor_tensor(nf[:, :, :], nf[:, :, :], ln1[:, :, :], ALU.subtract)
                    V.tensor_tensor(gg[:, :, :], gg[:, :, :], ln1[:, :, :], ALU.subtract)
                    dve.drain().then_inc(X.hg_ar, 1)
                    V.tensor_tensor_scan(run[:, 0, :], run_mask[:, :], gg[:, 0, :], 0.0, ALU.mult, ALU.add)
                    V.tensor_tensor_scan(run[:, 1, ::-1], run_mask[:, :], gg[:, 1, ::-1], 0.0, ALU.mult, ALU.add)
                    dve.drain()
                    V.tensor_tensor(rc(qk64[:, 2, :]), rc(run[:, 0, :])[:, :, CS - 1:CS].broadcast_to([P, NC, CS]),
                                    rc(run[:, 0, :]), ALU.subtract)
                    V.tensor_tensor(rc(qk64[:, 3, :]), rc(run[:, 1, :])[:, :, 0:1].broadcast_to([P, NC, CS]),
                                    rc(run[:, 1, :]), ALU.subtract)
                    dve.drain().then_inc(X.hg_rem, 1)
                    dve.wait_ge(X.hg_kexp, u + 1)
                    V.tensor_scalar(kk[:, :, :], kk[:, :, :], lb_h[:, 1:2], None, ALU.mult)
                    dve.drain()
                    V.tensor_tensor(k_sum[:, :], kk[:, 0, :], kk[:, 1, :], ALU.add)
                    level_sub(0)
                    level_sub(1)

                def head_decays(u):
                    dve.wait_ge(X.hg_stage, u + 1)
                    dve.wait_ge(X.hg_e, u + 1)
                    V.tensor_copy(tot[:, 0:8], rc(qk64[:, 0, :])[:, :, CS - 1])
                    V.tensor_copy(tot[:, 8:16], rc(qk64[:, 1, :])[:, :, 0])
                    dve.drain()
                    V.tensor_tensor(qk64[:, 0:2, :], qk64[:, 0:2, :],
                                    hq[:, :].rearrange("p (a n) -> p a n", a=1).broadcast_to([P, 2, SEQ]), ALU.mult)
                    V.tensor_tensor(qk64[:, 2:4, :], qk64[:, 2:4, :], kk[:, :, :], ALU.mult)
                    tv = tot.rearrange("p (a s) -> p a s", s=2)
                    V.tensor_tensor(ttot, tv[:, :, 0], tv[:, :, 1], ALU.mult)
                    dve.drain().then_inc(X.hg_q64, 1)

                def head(i, last):
                    u = l * 4 + i
                    dve.wait_ge(X.lev_mm, u * 8 + 1)
                    V.tensor_copy(ATd, bank[4][:, :].rearrange("p (a n) -> p a n", n=P))
                    dve.drain().then_inc(X.lev_taken, 1)
                    dve.wait_ge(X.lev_mm, u * 8 + 2)
                    b5 = bank[5][:, :].rearrange("p (a n) -> p a n", n=P)
                    V.tensor_copy(ATd[0:CS, :, CS:P], b5[0:CS, :, CS:P])
                    V.tensor_copy(ATd[CS:P, :, 0:CS], b5[CS:P, :, 0:CS])
                    dve.drain().then_inc(X.lev_taken, 1)
                    r4 = lambda t: t.rearrange("p (a s n) -> p a s n", s=2, n=CS)
                    for row, outer, d in ((0, 1, 0), (2, 0, 0), (1, 0, 1), (3, 1, 1)):
                        t_in = tot[:, 8 * d:8 * d + 8].rearrange("p (a s) -> p a s", s=2)[:, :, 1 - outer:2 - outer]
                        v = r4(qk64[:, row, :])[:, :, outer, :]
                        V.tensor_tensor(v, v, t_in.broadcast_to([P, TT_, CS]), ALU.mult)
                    dve.drain()
                    sc = lambda d, t: ttot[:, 4 * d + t:4 * d + t + 1]
                    V.tensor_scalar(q_far[:, 0, :], qk64[:, 0, sl(2)], sc(0, 1), None, ALU.mult)
                    V.tensor_scalar(q_far[:, 1, :], qk64[:, 0, sl(3)], sc(0, 2), None, ALU.mult)
                    V.tensor_scalar(q_far[:, 3, :], qk64[:, 1, sl(1)], sc(1, 2), None, ALU.mult)
                    V.tensor_scalar(q_far[:, 4, :], qk64[:, 1, sl(0)], sc(1, 1), None, ALU.mult)
                    dve.drain()
                    V.tensor_scalar(q_far[:, 2, :], q_far[:, 1, :], sc(0, 1), None, ALU.mult)
                    V.tensor_scalar(q_far[:, 5, :], q_far[:, 4, :], sc(1, 2), None, ALU.mult)
                    dve.drain().then_inc(X.hg_q128, 1)
                    for j in range(len(LEVELS)):
                        level_mul(u, j)
                        if j + 2 < len(LEVELS):
                            level_sub(j + 2)
                        if j >= 1:
                            level_take(u, j - 1)
                    level_take(u, len(LEVELS) - 1)
                    if not last:
                        head_gates(i + 1, u + 1, l * CH + (C_P2 + H0 + 2 + 4) + i * 8)
                    dve.wait_ge(X.hg_og, u + 1)
                    V.scalar_tensor_tensor(og_t[:, :], og_t[:, :], 1.0, tile_of(z, i + 20), ALU.add, ALU.mult)
                    inverse_rms(P, bank[7], X.hg_ms, X.hg_rt, X.hg_rc, u, X.hg_st)
                    if not last:
                        head_decays(u + 1)
                    dve.wait_ge(X.hg_bc, u + 1)
                    V.scalar_tensor_tensor(ho_f[:, :], ho_f[:, :], par[:, G_HG:G_HG + 1], bank[7][:, :],
                                           ALU.mult, ALU.mult)
                    dve.drain()
                    V.tensor_tensor(ho_f[:, :], ho_f[:, :], og_t[:, :], ALU.mult)
                    dve.drain()
                    split(tile_of(yc_hi, i), tile_of(yc_lo, i), ho_f[:, :])
                    dve.drain().then_inc(X.hg_out, 1)

                head_gates(0, l * 4, l * CH + (C_P1 + 2 + 4))
                head_decays(l * 4)
                with dve.Fori(0, 3) as i:
                    head(i, False)
                head(3, True)
                A = att["a"]
                with dve.Fori(0, 4) as i:
                    u = l * 4 + i
                    row_max("a", u, 1, (i + 24, i + 28))
                    V.tensor_scalar(p_c2, p_rs[:, 4:8], par[:, NLAM:NLAM + 1], None, ALU.mult)
                    for t0 in (0, 2):
                        for t in (t0, t0 + 1):
                            V.tensor_scalar(S[:, 0, t, :], S[:, 0, t, :], p_rs[:, t:t + 1], None, ALU.mult)
                        dve.drain()
                        for t in (t0, t0 + 1):
                            V.scalar_tensor_tensor(S[:, 0, t, :], S[:, 1, t, :], p_c2[:, t:t + 1], S[:, 0, t, :],
                                                   ALU.mult, ALU.add).then_inc(A["pd"], 1)
                    take(l, C_P3, i, 0, 0, i + 36)
                    gated_sum(l, C_P3, i, 1, 3, l * 24 + i * 2, i * 2, "first")
                    take(l, C_P3, i, 2, 1, i + 40)
                    inverse_rms(P, bank[5], A["ms"], A["rt"], A["rc"], u, A["st"])
                    dve.wait_ge(A["bc"], u + 1)
                    V.scalar_tensor_tensor(o_f[:, :], o_f[:, :], par[:, G_SUB:G_SUB + 1], bank[7][:, :],
                                           ALU.mult, ALU.mult)
                    dve.drain()
                    split(tile_of(ya_hi, i), tile_of(ya_lo, i), o_f[:, :])
                    dve.drain().then_inc(A["out"], 1)
                    gated_sum(l, C_P3, i, 3, 3, l * 24 + i * 2 + 1, i * 2 + 1, "first")
                B = att["b"]
                with dve.Fori(0, 2) as i:
                    for r in range(2):
                        u = l * 4 + i * 2 + r
                        p = i * 2 + r
                        row_max("b", u, 2, (p * 5 + 4, p + 36))
                        for g in range(8):
                            V.tensor_scalar(S[:, g // 4, g % 4, :], S[:, g // 4, g % 4, :], p_rs[:, g:g + 1],
                                            None, ALU.mult).then_inc(B["pd"], 1)
                        gated_sum(l, C_P4, i, 2 * r, 1, l * 24 + i * 4 + (8 + 2 * r), i * 4 + 2 * r, "more")
                        gated_sum(l, C_P4, i, 2 * r + 1, 3, l * 24 + i * 4 + (9 + 2 * r), i * 4 + 2 * r + 1, "more")
                        dve.wait_ge(B["pv"], u + 1)
                        split(tile_of(yb_hi, i * 2 + r), tile_of(yb_lo, i * 2 + r), bank[4][:, :])
                        dve.drain().then_inc(B["out"], 1)
                with dve.Fori(0, 2) as i:
                    for c in range(4):
                        gated_sum(l, C_P5, i, c, 2 * (c % 2) + 1, l * 24 + i * 4 + (16 + c), i * 4 + c, "last")
                V.memset(sq_sum[:, :], 0.0)
                dve.drain()
                dve.wait_ge(X.h_back, l * 16 + 16)
                dve.nop(nofuse=True)
                with dve.Fori(0, 2) as i:
                    for c in range(4):
                        dve.wait_ge(X.chunk_done, l * CH + (C_P6 + c + 3) + i * 4)
                        hj = tile_of(h, i * 4 + c)
                        V.tensor_tensor(hj, bank[c][:, :], hj, ALU.add).then_inc(X.h_upd, 1)
                        dve.drain().then_inc(X.prod_taken, 1)
                        add_square(c % 2, l * 24 + i * 4 + (16 + c))
                norm(l * 3 + 2, G_FFN2)
                ffn(l, 1)
            nu = DEPTH * 3
            inverse_rms(D, bank[7], X.n_ms, X.n_rt, X.n_rc, nu, X.n_stat)
            dve.wait_ge(X.n_bc, nu + 1)
            for k in range(KD):
                V.scalar_tensor_tensor(h_out[:, k, :], h[:, k, :], fin_g[:, k:k + 1], bank[6][:, :],
                                       ALU.mult, ALU.mult).then_inc(X.out_ready, 1)


def alibi_tables():
    n = 12
    slopes = np.exp2(np.float32(-8.0) * np.arange(1, n + 1, dtype=np.float32) / np.float32(n)).astype(np.float32)
    d = np.arange(UW)[None, :] - 384 - np.arange(P)[:, None]
    dist = np.abs(d)
    count = np.zeros(d.shape, np.int64)
    for window, dilation in ((128, 1), (512, 4), (2048, 16)):
        count += (dist % dilation == 0) & (dist // dilation <= window // (2 * dilation))
    ln_count = np.where(count > 0, np.log(np.maximum(count, 1)), -1e30)
    out = np.zeros((n, P, UW), np.float32)
    for row, s in enumerate((0, 3, 6, 9, 1, 2, 4, 5, 7, 8, 10, 11)):
        b = (-slopes[s] * dist.astype(np.float32)).astype(np.float64)
        out[row] = ((b + (ln_count if row >= 4 else 0)) / SCALE).astype(np.float32)
    return out


def level_masks():
    s, t = np.arange(P)[:, None], np.arange(P)[None, :]
    rows = [((s // (2 * m) == t // (2 * m)) & (s // m != t // m)) for m in LEVELS]
    return np.concatenate(rows, axis=1).astype(np.float32)


def kernel(**inputs):
    import concourse.bacc as bacc
    from concourse.bass_utils import run_bass_kernel_spmd

    a = {k: np.asarray(v) for k, v in inputs.items()}

    def blocks(w, cols):
        k, n = w.shape
        b = w.reshape(k // P, P, n // P, P).transpose(2, 1, 0, 3)
        return b[cols]

    def chunks(w, cols):
        b = blocks(w, cols)
        return b.reshape(b.shape[0], P, -1)

    gu, dn, proj, mrg, wo = [], [], [], [], []
    order = []
    for i in range(4):
        order += [28 + i, 32 + i, 24 + i, 36 + i, 40 + i, i, 4 + i] + [7 + i] * (i > 0)
    order += [12, 13, 14, 15, 11]
    for i in range(4):
        order += [16 + i, 20 + i]
    for l in range(DEPTH):
        for f in ("ffn1", "ffn2"):
            g = chunks(a[f + "_w_gate"][l], slice(None))
            u = chunks(a[f + "_w_up"][l], slice(None))
            gu.append(np.stack([g, u], axis=1).reshape(-1, P, D))
            d = blocks(a[f + "_w_down"][l], slice(None)).reshape(KD, P, 2, HALF * P).transpose(0, 2, 1, 3)
            dn.append(d.reshape(-1, P, HALF * P))
        proj.append(chunks(a["w_in"][l], order))
        gates = chunks(a["w_in"][l], slice(44, 68)).reshape(3, KD, P, D)
        for b, name in ((2, "w_branch_c"), (0, "w_branch_a"), (1, "w_branch_b")):
            mrg.append(np.concatenate([gates[b], chunks(a[name][l], slice(None))], axis=2))
        wo.append(chunks(a["w_out"][l], slice(None)))
    per_p = lambda v: v.reshape(DEPTH, -1, P).transpose(2, 0, 1)
    gains = np.concatenate([per_p(a[n]) for n in ("ffn1_norm", "mix_norm", "ffn2_norm", "diff_subln", "hgrn_norm")],
                           axis=2)
    lam_in = np.concatenate([a["diff_lambda_" + n].T for n in ("q1", "k1", "q2", "k2")], axis=1)
    arrays = {
        "xT": a["x"][0].T, "wgu": np.concatenate(gu), "wdn": np.concatenate(dn),
        "wproj": np.concatenate(proj), "wmerge": np.concatenate(mrg), "wout": np.concatenate(wo),
        "gains": gains, "final_g": a["final_norm"].reshape(KD, P).T,
        "lb_raw": per_p(a["hgrn_lower_bounds"]).reshape(P, -1), "lam_in": lam_in,
        "ident": np.eye(P, dtype=np.float32), "masks": level_masks(), "bias": alibi_tables(),
    }
    arrays = {k: np.ascontiguousarray(v) for k, v in arrays.items()}

    nc = bacc.Bacc("TRN2", target_bir_lowering=False, num_devices=1, dynamic_dma_scratch_size=1024)
    aps = [nc.dram_tensor("in_" + k, v.shape, mybir.dt.from_np(v.dtype), kind="ExternalInput").ap()
           for k, v in arrays.items()]
    h_save = nc.dram_tensor("h_save", (D, SEQ), F32, kind="Internal").ap()
    out = nc.dram_tensor("out_T", (D, SEQ), F32, kind="ExternalOutput").ap()
    build(nc, *aps, h_save, out)
    r = run_bass_kernel_spmd(nc, [{"in_" + k: v for k, v in arrays.items()}], core_ids=[0])
    return np.ascontiguousarray(r.results[0]["out_T"].T)[None]
```
